# Optimizing a Trainium2 kernel written in Bass

```python
import math
import jax, jax.numpy as jnp
from jax import lax
import numpy as np

D_MODEL = 1024
BATCH = 1
SEQ = 256
DEPTH = 2

MEM_LEN = 256

SSD_HEAD_DIM = 64
SSD_INNER = D_MODEL
SSD_HEADS = SSD_INNER // SSD_HEAD_DIM
SSD_GROUPS = 2
SSD_STATE = 64
SSD_CONV = 4
SSD_CHUNK = 128
SSD_CONV_DIM = SSD_INNER + 2 * SSD_GROUPS * SSD_STATE

SB_HEADS = 8
SB_HEAD_DIM = 64
SB_WIDTH = SB_HEADS * SB_HEAD_DIM
SB_BLOCK = 128

XA_HEADS = 4
XA_HEAD_DIM = 128
XA_WIDTH = XA_HEADS * XA_HEAD_DIM

D_FF = 2816
N_EXPERTS = 8
TOP_K = 2
N_DENSE = (DEPTH + 1) // 2
N_MOE = DEPTH // 2

IN_WIDTH = SSD_INNER + SSD_CONV_DIM + SSD_HEADS + 3 * SB_WIDTH + 2 * D_MODEL
EPS = 1e-6

kernel_name = "hybrid_ssd_stickbreaking_moe_trunk"

def rmsnorm(x, g):
    xf = x.astype(jnp.float32)
    y = xf * lax.rsqrt(jnp.mean(xf * xf, axis=-1, keepdims=True) + EPS)
    return (y * g.astype(jnp.float32)).astype(x.dtype)

def causal_dwconv(x, w, b):
    S = x.shape[1]
    K = w.shape[0]
    xp = jnp.pad(x, ((0, 0), (K - 1, 0), (0, 0)))
    y = b
    for k in range(K):
        y = y + xp[:, k:k + S] * w[k]
    return y

def ssd_branch(z, xbc, dt_raw, conv_w, conv_b, dt_bias, a_log, d_skip, norm_g):
    Bsz, S, _ = xbc.shape
    G, hg, P, N, L = SSD_GROUPS, SSD_HEADS // SSD_GROUPS, SSD_HEAD_DIM, SSD_STATE, SSD_CHUNK
    nc = S // L
    xbc = jax.nn.silu(causal_dwconv(xbc, conv_w, conv_b))
    xs, Bm, Cm = jnp.split(xbc, [SSD_INNER, SSD_INNER + G * N], axis=-1)
    x = xs.reshape(Bsz, nc, L, G, hg, P)
    Bm = Bm.reshape(Bsz, nc, L, G, N)
    Cm = Cm.reshape(Bsz, nc, L, G, N)
    dt = jax.nn.softplus((dt_raw + dt_bias).astype(jnp.float32))
    a = (dt * -jnp.exp(a_log.astype(jnp.float32))).reshape(Bsz, nc, L, G, hg)
    xdt = x * dt.reshape(Bsz, nc, L, G, hg)[..., None].astype(x.dtype)
    a_cum = jnp.cumsum(a, axis=2)
    causal = jnp.tril(jnp.ones((L, L), dtype=bool))
    seg = a_cum[:, :, :, None] - a_cum[:, :, None, :]
    decay = jnp.exp(jnp.where(causal[:, :, None, None], seg, -jnp.inf))
    cb = jnp.einsum('bctgn,bcsgn->bctsg', Cm, Bm)
    y_diag = jnp.einsum('bctsgh,bcsghp->bctghp', (cb[..., None] * decay).astype(x.dtype), xdt)
    decay_to_end = jnp.exp(a_cum[:, :, -1:] - a_cum)
    states = jnp.einsum('bclgn,bclghp->bcghpn', Bm, xdt * decay_to_end[..., None].astype(x.dtype))
    chunk_decay = jnp.exp(a_cum[:, :, -1]).astype(states.dtype)

    def step(carry, inp):
        st, dec = inp
        return carry * dec[..., None, None] + st, carry

    _, prev = lax.scan(step, jnp.zeros_like(states[:, 0]),
                       (jnp.moveaxis(states, 1, 0), jnp.moveaxis(chunk_decay, 1, 0)))
    prev = jnp.moveaxis(prev, 0, 1)
    y_off = jnp.einsum('bctgn,bcghpn->bctghp', Cm, prev) * jnp.exp(a_cum)[..., None].astype(x.dtype)
    y = y_diag + y_off + x * d_skip.reshape(G, hg)[:, :, None]
    y = y.reshape(Bsz, S, SSD_INNER) * jax.nn.silu(z)
    y = rmsnorm(y.reshape(Bsz, S, G, SSD_INNER // G), norm_g.reshape(G, SSD_INNER // G))
    return y.reshape(Bsz, S, SSD_INNER)

def stick_breaking_attention(qkv):
    Bsz, S, _ = qkv.shape
    q, k, v = jnp.split(qkv, 3, axis=-1)
    q = q.reshape(Bsz, S, SB_HEADS, SB_HEAD_DIM).transpose(0, 2, 1, 3)
    k = k.reshape(Bsz, S, SB_HEADS, SB_HEAD_DIM).transpose(0, 2, 1, 3)
    v = v.reshape(Bsz, S, SB_HEADS, SB_HEAD_DIM).transpose(0, 2, 1, 3)
    scale = SB_HEAD_DIM ** -0.5
    outs = []
    for blk in range(S // SB_BLOCK):
        t0 = blk * SB_BLOCK
        t1 = t0 + SB_BLOCK
        zb = jnp.einsum('bhtd,bhsd->bhts', q[:, :, t0:t1], k[:, :, :t1]).astype(jnp.float32) * scale
        t_idx = t0 + jnp.arange(SB_BLOCK)
        s_idx = jnp.arange(t1)
        mask = s_idx[None, :] < t_idx[:, None]
        log_keep = jnp.where(mask, jax.nn.log_sigmoid(-zb), 0.0)
        log_between = lax.cumsum(log_keep, axis=3, reverse=True) - log_keep
        att = jnp.where(mask, jnp.exp(jax.nn.log_sigmoid(zb) + log_between), 0.0)
        outs.append(jnp.einsum('bhts,bhsd->bthd', att.astype(v.dtype), v[:, :, :t1]))
    return jnp.concatenate(outs, axis=1).reshape(Bsz, S, SB_WIDTH)

def cross_attention(h, mem_n, wq, wk, wv, wo):
    Bsz, S, _ = h.shape
    M = mem_n.shape[1]
    q = (h @ wq).reshape(Bsz, S, XA_HEADS, XA_HEAD_DIM)
    k = (mem_n @ wk).reshape(Bsz, M, XA_HEADS, XA_HEAD_DIM)
    v = (mem_n @ wv).reshape(Bsz, M, XA_HEADS, XA_HEAD_DIM)
    s = jnp.einsum('bshd,bmhd->bhsm', q, k).astype(jnp.float32) * (XA_HEAD_DIM ** -0.5)
    p = jax.nn.softmax(s, axis=-1).astype(v.dtype)
    o = jnp.einsum('bhsm,bmhd->bshd', p, v).reshape(Bsz, S, XA_WIDTH)
    return o @ wo

def swiglu(u, w_gate, w_up, w_down):
    return (jax.nn.silu(u @ w_gate) * (u @ w_up)) @ w_down

def moe_ffn(u, w_router, w_gate, w_up, w_down):
    logits = (u @ w_router).astype(jnp.float32)
    top_val, top_idx = lax.top_k(logits, TOP_K)
    top_w = jax.nn.softmax(top_val, axis=-1)
    combine = jnp.sum(jax.nn.one_hot(top_idx, N_EXPERTS, dtype=jnp.float32) * top_w[..., None],
                      axis=-2).astype(u.dtype)
    out = jnp.zeros_like(u)
    for e in range(N_EXPERTS):
        out = out + combine[..., e:e + 1] * swiglu(u, w_gate[e], w_up[e], w_down[e])
    return out

def setup_inputs(seed: int = 0) -> dict:
    key = jax.random.key(seed)
    ks = jax.random.split(key, 32)

    def dense(k, shape, fan_in):
        return jax.random.normal(k, shape, jnp.float32) * (fan_in ** -0.5)

    def gain(k, shape):
        return 1.0 + 0.05 * jax.random.normal(k, shape, jnp.float32)

    dt0 = jnp.exp(jax.random.uniform(ks[7], (DEPTH, SSD_HEADS), jnp.float32,
                                     math.log(1e-3), math.log(1e-1)))
    return {
        "x": jax.random.normal(ks[0], (BATCH, SEQ, D_MODEL), jnp.float32),
        "mem": jax.random.normal(ks[1], (BATCH, MEM_LEN, D_MODEL), jnp.float32),
        "norm_mix": gain(ks[2], (DEPTH, D_MODEL)),
        "w_in": dense(ks[3], (DEPTH, D_MODEL, IN_WIDTH), D_MODEL),
        "conv_w": dense(ks[4], (DEPTH, SSD_CONV, SSD_CONV_DIM), SSD_CONV),
        "conv_b": 0.02 * jax.random.normal(ks[5], (DEPTH, SSD_CONV_DIM), jnp.float32),
        "dt_bias": dt0 + jnp.log(-jnp.expm1(-dt0)),
        "a_log": jnp.log(jax.random.uniform(ks[8], (DEPTH, SSD_HEADS), jnp.float32, 1.0, 16.0)),
        "d_skip": gain(ks[9], (DEPTH, SSD_HEADS)),
        "ssd_norm": gain(ks[10], (DEPTH, SSD_INNER)),
        "w_ssd_o": dense(ks[11], (DEPTH, SSD_INNER, D_MODEL), SSD_INNER),
        "w_sb_o": dense(ks[12], (DEPTH, SB_WIDTH, D_MODEL), SB_WIDTH),
        "w_out": dense(ks[13], (DEPTH, D_MODEL, D_MODEL), D_MODEL),
        "norm_xa": gain(ks[14], (DEPTH, D_MODEL)),
        "norm_mem": gain(ks[15], (DEPTH, D_MODEL)),
        "xa_wq": dense(ks[16], (DEPTH, D_MODEL, XA_WIDTH), D_MODEL),
        "xa_wk": dense(ks[17], (DEPTH, D_MODEL, XA_WIDTH), D_MODEL),
        "xa_wv": dense(ks[18], (DEPTH, D_MODEL, XA_WIDTH), D_MODEL),
        "xa_wo": dense(ks[19], (DEPTH, XA_WIDTH, D_MODEL), XA_WIDTH),
        "norm_ffn": gain(ks[20], (DEPTH, D_MODEL)),
        "ffn_w_gate": dense(ks[21], (N_DENSE, D_MODEL, D_FF), D_MODEL),
        "ffn_w_up": dense(ks[22], (N_DENSE, D_MODEL, D_FF), D_MODEL),
        "ffn_w_down": dense(ks[23], (N_DENSE, D_FF, D_MODEL), D_FF),
        "moe_router": dense(ks[24], (N_MOE, D_MODEL, N_EXPERTS), D_MODEL),
        "moe_w_gate": dense(ks[25], (N_MOE, N_EXPERTS, D_MODEL, D_FF), D_MODEL),
        "moe_w_up": dense(ks[26], (N_MOE, N_EXPERTS, D_MODEL, D_FF), D_MODEL),
        "moe_w_down": dense(ks[27], (N_MOE, N_EXPERTS, D_FF, D_MODEL), D_FF),
        "final_norm": gain(ks[28], (D_MODEL,)),
    }

def reference(x, mem, norm_mix, w_in, conv_w, conv_b, dt_bias, a_log, d_skip, ssd_norm,
              w_ssd_o, w_sb_o, w_out, norm_xa, norm_mem, xa_wq, xa_wk, xa_wv, xa_wo,
              norm_ffn, ffn_w_gate, ffn_w_up, ffn_w_down, moe_router, moe_w_gate,
              moe_w_up, moe_w_down, final_norm):
    offsets = [SSD_INNER,
               SSD_INNER + SSD_CONV_DIM,
               SSD_INNER + SSD_CONV_DIM + SSD_HEADS,
               SSD_INNER + SSD_CONV_DIM + SSD_HEADS + 3 * SB_WIDTH,
               SSD_INNER + SSD_CONV_DIM + SSD_HEADS + 3 * SB_WIDTH + D_MODEL]
    h = x
    for i in range(DEPTH):
        u = rmsnorm(h, norm_mix[i])
        proj = u @ w_in[i]
        z, xbc, dt_raw, qkv, g_ssd, g_sb = jnp.split(proj, offsets, axis=-1)
        y_ssd = ssd_branch(z, xbc, dt_raw, conv_w[i], conv_b[i], dt_bias[i], a_log[i],
                           d_skip[i], ssd_norm[i])
        y_sb = stick_breaking_attention(qkv)
        merged = (jax.nn.sigmoid(g_ssd) * (y_ssd @ w_ssd_o[i])
                  + jax.nn.sigmoid(g_sb) * (y_sb @ w_sb_o[i]))
        h = h + merged @ w_out[i]
        h = h + cross_attention(rmsnorm(h, norm_xa[i]), rmsnorm(mem, norm_mem[i]),
                                xa_wq[i], xa_wk[i], xa_wv[i], xa_wo[i])
        u = rmsnorm(h, norm_ffn[i])
        j = i // 2
        if i % 2 == 0:
            h = h + swiglu(u, ffn_w_gate[j], ffn_w_up[j], ffn_w_down[j])
        else:
            h = h + moe_ffn(u, moe_router[j], moe_w_gate[j], moe_w_up[j], moe_w_down[j])
    return rmsnorm(h, final_norm)


_drawn_inputs = setup_inputs


def setup_inputs(seed=0):
    import zlib

    import numpy as np

    out = dict(_drawn_inputs(seed))
    spreads = {}
    factors = {'norm_xa': 5.934, 'norm_mem': 4.472}
    for name, (base, spread) in spreads.items():
        noise = np.random.default_rng([zlib.crc32(name.encode()), seed]).standard_normal(out[name].shape)
        drawn = base * np.exp(spread * noise) if base else spread * noise
        out[name] = __import__('jax').numpy.asarray(drawn.astype(out[name].dtype))
    for name, factor in factors.items():
        out[name] = (out[name] * factor).astype(out[name].dtype)
    return out
```

```python
from contextlib import ExitStack

import numpy as np
import concourse.bass as bass
from concourse import mybir
from concourse.alu_op_type import AluOpType as ALU

F32 = mybir.dt.float32
F32R = mybir.dt.float32r
I32 = mybir.dt.int32
ACT = mybir.ActivationFunctionType
AX = mybir.AxisListType

P = 128
D = 1024
S = 256
NT = S // P
KD = D // P
DEPTH = 2
EPS = 1e-6
HEADS = 16
HD = 64
SBH = 8
XH = 4
CONV = 4
CT = 10
FF = 2816
NE = 8
CH = FF // 256
UNIT = 2048
RAW = 4
RAW_E = 7
HL = 3
NSEM = 11
EU = 3 * CH
XSCALE = 128.0 ** -0.5
SPACE = 207 * 1024

MIX = ([("q", j) for j in range(2)] + [("k", j) for j in range(2)] + [("v", j) for j in range(2)]
       + [("xbc", j) for j in (4, 0, 1, 2, 3)] + [("ga", j) for j in range(4)] + [("gb", j) for j in range(4)]
       + [("z", j) for j in range(4)] + [("sbo", j) for j in range(2)] + [("ssdo", j) for j in range(4)]
       + [("wout", j) for j in range(4)] + [("xk", j) for j in range(2)] + [("xv", j) for j in range(2)]
       + [("xq", j) for j in range(2)] + [("xo", j) for j in range(2)])
NMIX = len(MIX)
FFN0 = NMIX
LAYER1 = FFN0 + EU
MOE0 = LAYER1 + NMIX
NUNITS = MOE0 + NE * EU
UNIT_OF = {(l, *m): (0, LAYER1)[l] + i for l in range(DEPTH) for i, m in enumerate(MIX)}

BY_DVE = ("sbo", "ssdo", "wout", "xo")
OUTS = [(l, n, j, part) for l in range(DEPTH) for n, j in MIX for part in range(2 if n in ("sbo", "xo") else 1)]
OUT_NO = {o: i for i, o in enumerate(OUTS)}


def slot_of(u):
    return (u - MOE0) % RAW if u < MOE0 else (u - MOE0 + RAW) % RAW_E


def out_reader(i):
    dve = OUTS[i][1] in BY_DVE
    return dve, sum((o[1] in BY_DVE) == dve for o in OUTS[:i + 1])


N_MIX, N_SSD, N_MEM, N_XA, N_FFN = range(5)
NNORM = 5


def trunk(nc, x, mem, units, w_dt, w_router, gains, convw, rows, ffn_row, final_row, out):
    ctx = ExitStack()
    with ctx:
        space = ctx.enter_context(nc.sbuf_tensor("space", [P, SPACE // 4], F32))
        base = nc.sbuf_base - SPACE
        at, top = {}, [0]

        def sb(name, shape, dt=F32, over=None, skip=0):
            size = 4 * int(np.prod(shape[1:]))
            size = (size + 31) // 32 * 32
            if over is None:
                at[name] = top[0]
                top[0] += size
                assert top[0] <= SPACE, (name, top[0])
            else:
                at[name] = at[over] + skip
            return nc.alloc_sbuf_tensor_at(name, shape, dt, offset=base + at[name])

        def sem(name):
            return ctx.enter_context(nc.semaphore(name))

        raw = sb("raw", [P, RAW, UNIT])
        raw_e = sb("raw_e", [P, RAW_E, UNIT], over="raw")
        xpad = sb("xpad", [P, CT * (S + CONV - 1)])
        zs = sb("zs", [P, 2, NT, 256])
        cbm = sb("cbm", [P, 2, 2, P])
        xtok = sb("xtok", [P, NT, D])
        assert at["xtok"] >= at["raw"] + 4 * UNIT * (RAW_E - 1) and RAW_E * UNIT * 4 <= at["xtok"] + 4 * NT * D
        whi = sb("whi", [P, HL, UNIT], F32R)
        wlo = sb("wlo", [P, HL, UNIT], F32R)
        u_hi = sb("u_hi", [P, KD, S], F32R)
        u_lo = sb("u_lo", [P, KD, S], F32R)
        m_hi = sb("m_hi", [P, KD, S], F32R)
        m_lo = sb("m_lo", [P, KD, S], F32R)
        o_hi = sb("o_hi", [P, 4, S], F32R)
        o_lo = sb("o_lo", [P, 4, S], F32R)
        h = sb("h", [P, NT, D])
        xn = sb("xn", [P, NT, D])
        xc = sb("xc", [P, CT, S])
        qk = sb("qk", [P, 8, S])
        sbw = sb("sbw", [P, 3, 2, 384])
        sbl, sbp, sba = sbw[:, 0], sbw[:, 1], sbw[:, 2]
        gb = sb("gb", [P, KD, S])
        hT_hi = sb("hT_hi", [P, 2, 2, S], F32R, over="qk")
        hT_lo = sb("hT_lo", [P, 2, 2, S], F32R, over="qk", skip=4096)
        sel = sb("sel", [P, NT, P], F32R, over="gb")
        selT = sb("selT", [P, S], F32R, over="gb", skip=2048)
        wdt = sb("wdt", [P, KD * 16])
        wdt_hi = sb("wdt_hi", [P, KD * 16], F32R)
        wdt_lo = sb("wdt_lo", [P, KD * 16], F32R)
        wr = sb("wr", [P, KD * NE])
        wr_hi = sb("wr_hi", [P, KD * NE], F32R)
        wr_lo = sb("wr_lo", [P, KD * NE], F32R)
        gain = sb("gain", [P, DEPTH * NNORM * KD])
        cw = sb("cw", [P, DEPTH * CT * (CONV + 1)])
        row = sb("row", [P, DEPTH * 3 * HEADS])
        ident = sb("ident", [P, P])
        tri_le = sb("tri_le", [P, P])
        tri_gt = sb("tri_gt", [P, P])
        neg_ge = sb("neg_ge", [P, P])
        tri_lt = sb("tri_lt", [P, P])
        neg_one = sb("neg_one", [P, P])
        one = sb("one", [P, P])
        iota = sb("iota", [P, P])
        first = sb("first", [P, NE])
        ss = sb("ss", [P, 64])
        rs = sb("rs", [P, 64])
        half = sb("half", [P, 4])
        sdt = sb("sdt", [P, 7, NT, HEADS])
        eacum = sb("eacum", [P, 2, HEADS])
        btok = sb("btok", [P, P])
        xmx = sb("xmx", [P, 4, XH, NT])
        rt = sb("rt", [P, 12, NT, NE])
        rt1 = sb("rt1", [P, 8, NT])
        rank2 = sb("rank2", [P, NT, 2 * NE + 1])
        mask2 = sb("mask2", [P, NT, 2 * NE + 1])
        comb2 = sb("comb2", [P, NT, 2 * NE + 1])
        wslot = sb("wslot", [P, 1])
        visits = sb("visits", [P, 4])
        visits_i = sb("visits_i", [P, 1], I32)

        ps = ctx.enter_context(nc.psum_tensor("ps", [P, 8, 512], F32))

        def flat(t):
            return t[:, :, :].rearrange("p a b -> p (a b)")

        xdt = xpad[:, 0:NT * D].rearrange("p (t f) -> p t f", t=NT)
        prev = xpad[:, NT * D:NT * D + 512]
        merged = xpad[:, 0:KD * S].rearrange("p (k s) -> p k s", k=KD)
        xconv = xpad[:, :].rearrange("p (c s) -> p c s", c=CT)
        decay = xc[:, 0:8, :].rearrange("p a (b t) -> p (a b) t", t=P)
        atri = qk[:, :, :].rearrange("p a (b t) -> p (a b) t", t=P)
        va = zs[:, :, :, :].rearrange("p a b c -> p (a b c)").rearrange("p (t f) -> p t f", t=NT)
        ga = sbw[:, :, :, :].rearrange("p a b c -> p (a b c)")[:, 0:KD * S].rearrange("p (k s) -> p k s", k=KD)
        xdte = flat(gb)[:, 0:D]
        yoff = flat(gb)[:, D:2 * D]
        kx, qx = xc[:, 0:4, :], xc[:, 4:8, :]
        vx = flat(qk)[:, 0:1024].rearrange("p (t f) -> p t f", t=NT)
        pT = qk[:, 4:8, :]
        prob = gb
        grow = flat(xc)[:, 0:D]
        frow = flat(xc)[:, D:2 * D]
        mt_hi = flat(m_hi).rearrange("p (t f) -> p t f", t=NT)
        mt_lo = flat(m_lo).rearrange("p (t f) -> p t f", t=NT)
        ue_hi = o_hi[:, :, :].rearrange("p a (b c) -> p (a b) c", c=P)
        ue_lo = o_lo[:, :, :].rearrange("p a (b c) -> p (a b) c", c=P)
        y_hi, y_lo = flat(u_hi)[:, 0:D], flat(u_lo)[:, 0:D]
        sg = sbl[:, :, 0:256]
        act_f = sbp[:, :, 0:256]

        landed = [sem(f"landed{i}") for i in range(NSEM)]
        hi_made, lo_made, unit_used = sem("hi_made"), sem("lo_made"), sem("unit_used")
        half_unit, unit_begun = sem("half_unit"), sem("unit_begun")
        out_read_act, out_read_dve = sem("out_read_act"), sem("out_read_dve")
        params_in, h_in, mem_in = sem("params_in"), sem("h_in"), sem("mem_in")
        grow_in, frow_in = sem("grow_in"), sem("frow_in")
        consts = sem("consts")
        small_hi, small_lo = sem("small_hi"), sem("small_lo")
        small_raw, small_raw1 = sem("small_raw"), sem("small_raw1")
        sumsq, rstd, normed = sem("sumsq"), sem("rstd"), sem("normed")
        turned, turned_hi, turned_lo = sem("turned"), sem("turned_hi"), sem("turned_lo")
        q_out, v_out, x_out = sem("q_out"), sem("v_out"), sem("x_out")
        sb_z, sb_ln, sb_sp, sb_lp, sb_exp, sb_att, sb_y = (sem(n) for n in
            ("sb_z", "sb_ln", "sb_sp", "sb_lp", "sb_exp", "sb_att", "sb_y"))
        sb_hi, sb_lo = sem("sb_hi"), sem("sb_lo")
        dt_ps, dt_sum, dt_ln, dt_a, dt_cum, dt_exp = (sem(n) for n in
            ("dt_ps", "dt_sum", "dt_ln", "dt_a", "dt_cum", "dt_exp"))
        padded, conved, silued = sem("padded"), sem("conved"), sem("silued")
        x_turned, x_tok, x_dt, b_turned, b_tok = (sem(n) for n in ("x_turned", "x_tok", "x_dt", "b_turned", "b_tok"))
        a_tri, seg, decayed, cb_made, m_made = (sem(n) for n in
            ("a_tri", "seg", "decayed", "cb_made", "m_made"))
        y_ps, y_skip, y_read, st_in, st_ps, st_out, yoff_ps, yoff_read, yoff_added = (sem(n) for n in
            ("y_ps", "y_skip", "y_read", "st_in", "st_ps", "st_out", "yoff_ps", "yoff_read", "yoff_added"))
        z_silu, z_mul = sem("z_silu"), sem("z_mul")
        gates = sem("gates")
        merged_sum, merged_hi, merged_lo = sem("merged_sum"), sem("merged_hi"), sem("merged_lo")
        h_ffn = sem("h_ffn")
        kvx_out, xs_ps, xs_max, xs_exp, xs_p, xp_turned, xp_out, xo_ps, xo_hi, xo_lo = (sem(n) for n in
            ("kvx_out", "xs_ps", "xs_max", "xs_exp", "xs_p", "xp_turned", "xp_out", "xo_ps", "xo_hi", "xo_lo"))
        gu_ps, f_silu, f_act, f_hi, f_lo = (sem(n) for n in
            ("gu_ps", "f_silu", "f_act", "f_hi", "f_lo"))
        r_ps, r_mask, r_exp, r_rank, r_done, ut_made, ut_hi = (sem(n) for n in
            ("r_ps", "r_mask", "r_exp", "r_rank", "r_done", "ut_made", "ut_hi"))
        sel_made, selT_ps, selT_out, ue_ps, ue_hi_out, ue_lo_out = (sem(n) for n in
            ("sel_made", "selT_ps", "selT_out", "ue_ps", "ue_hi_out", "ue_lo_out"))
        w_ps, w_out_s = sem("w_ps"), sem("w_out_s")
        e_silu, e_act, e_turn, e_hi, e_lo, e_yhi, e_ylo, e_sc, e_add = (sem(n) for n in
            ("e_silu", "e_act", "e_turn", "e_hi", "e_lo", "e_yhi", "e_ylo", "e_sc", "e_add"))
        final_made, stored = sem("final_made"), sem("stored")
        act_chain, dve_chain, pool_chain = sem("act_chain"), sem("dve_chain"), sem("pool_chain")

        def chain(eng, s):
            count = [0]

            def link(ins):
                count[0] += 1
                ins.then_inc(s, 1)
                eng.wait_ge(s, count[0])
            return link

        def gcol(l, n, k):
            i = (l * NNORM + n) * KD + k
            return gain[:, i:i + 1]

        def rowof(l, i):
            a = (l * 3 + i) * HEADS
            return row[:, a:a + HEADS]

        def sums_before(n):
            return 2 * n + 2 * ((n + NNORM - 1 - N_SSD) // NNORM)

        def down_unit(c):
            return 3 * c + 4 if c < CH - 1 else EU - 1

        def up_unit(c):
            return 3 * c if c else 1

        block = ctx.enter_context(nc.Block())

        @block.sync
        def _(sp):
            sp.dma_start(h[:, :, :], x.rearrange("(t p) d -> p t d", p=P)).then_inc(h_in, 16)
            sp.dma_start(gain[:, :], gains[:, :]).then_inc(params_in, 16)
            sp.dma_start(cw[:, :], convw[:, :]).then_inc(params_in, 16)
            sp.dma_start(row[:, :], rows.partition_broadcast(P)).then_inc(params_in, 16)
            sp.dma_start(wdt[:, :], w_dt[0]).then_inc(small_raw, 16)
            sp.dma_start(wr[:, :], w_router[:, :]).then_inc(params_in, 16)

            def load(u):
                if u < MOE0:
                    sp.dma_start(raw[:, slot_of(u), :], units[u]).then_inc(landed[u % NSEM], 16)
                else:
                    sp.dma_start(raw_e[:, slot_of(u), :], units[u]).then_inc(landed[u % NSEM], 16)

            def load_experts(first, groups):
                with sp.Fori(0, groups) as g:
                    for j in range(NSEM):
                        slot = sp.snap((g * NSEM + (first + j - MOE0 + RAW)) % RAW_E)
                        unit = sp.snap(g * NSEM + (first + j - (NE * EU if first >= NUNITS else 0)))
                        free = sp.snap(g * NSEM + (first + j - RAW_E + 1))
                        sp.wait_ge(lo_made, free)
                        sp.dma_start(raw_e[:, bass.ds(slot, 1), :], units[bass.ds(unit, 1)].rearrange("u p n -> p u n"))\
                            .then_inc(landed[(first + j) % NSEM], 16)

            for u in range(NSEM):
                if u >= RAW:
                    sp.wait_ge(lo_made, u - RAW + 1)
                load(u)
            with sp.Fori(1, MOE0 // NSEM) as g:
                for j in range(NSEM):
                    slot = sp.snap((g * NSEM + (j + RAW - MOE0 % RAW)) % RAW)
                    unit = sp.snap(g * NSEM + j)
                    free = sp.snap(g * NSEM + (j - RAW + 1))
                    sp.wait_ge(lo_made, free)
                    sp.dma_start(raw[:, bass.ds(slot, 1), :], units[bass.ds(unit, 1)].rearrange("u p n -> p u n"))\
                        .then_inc(landed[j], 16)
            for u in range(MOE0 // NSEM * NSEM, MOE0):
                sp.wait_ge(lo_made, u - RAW + 1)
                load(u)
            for u in range(MOE0, MOE0 + NSEM):
                sp.wait_ge(lo_made, u - RAW_E + 1)
                if slot_of(u) == RAW_E - 1 and u < MOE0 + RAW_E:
                    sp.wait_ge(e_add, 1)
                load(u)
            load_experts(MOE0 + NSEM, NE * EU // NSEM - 1)
            sp.wait_ge(r_done, 1)
            n_visits = sp.value_load(visits_i[0:1, 0:1], min_val=NE, max_val=2 * NE)
            with sp.If(n_visits > NE):
                load_experts(NUNITS, NE * EU // NSEM)
            sp.wait_ge(final_made, 2)
            sp.dma_start(out.rearrange("(t p) d -> p t d", p=P), xn[:, :, :]).then_inc(stored, 16)
            sp.wait_ge(stored, 16)

        @block.gpsimd
        def _(gp):
            link = chain(gp, pool_chain)
            gp.memset(half[:, :], -0.5).then_inc(consts, 1)
            for m, v in ((ident, 0.0), (tri_le, 1.0), (tri_gt, 1.0), (neg_ge, -1.0), (tri_lt, 1.0)):
                link(gp.memset(m[:, :], v))
            gp.memset(neg_one[:, :], -1.0).then_inc(consts, 1)
            gp.memset(one[:, :], 1.0).then_inc(consts, 1)
            for m, op, fill, step in ((ident, ALU.not_equal, 1.0, -1), (tri_le, ALU.is_ge, 0.0, 1),
                                      (tri_gt, ALU.is_gt, 0.0, -1), (neg_ge, ALU.is_ge, 0.0, -1),
                                      (tri_lt, ALU.is_gt, 0.0, 1)):
                gp.affine_select(out=m[:, :], in_=m[:, :], compare_op=op, fill=fill, base=0,
                                 pattern=[[step, P]], channel_multiplier=-step).then_inc(consts, 1)
            gp.iota(iota[:, :], pattern=[[1, P]], base=0, channel_multiplier=0,
                    allow_small_or_imprecise_dtypes=True).then_inc(consts, 1)
            gp.iota(first[:, :], pattern=[[-1, NE]], base=NE, channel_multiplier=0,
                    allow_small_or_imprecise_dtypes=True).then_inc(consts, 1)
            gp.wait_ge(consts, 10)

            def root(n, cols, width):
                gp.wait_ge(sumsq, sums_before(n) + cols)
                c = slice(4 * n, 4 * n + cols)
                link(gp.tensor_scalar(ss[:, c], ss[:, c], 1.0 / width, EPS, ALU.mult, ALU.add))
                gp.tensor_tensor(out=rs[:, c], in0=ss[:, c], in1=half[:, 0:cols], op=ALU.pow).then_inc(rstd, 1)

            for l in range(DEPTH):
                root(l * NNORM + N_MIX, 2, D)
                if l:
                    gp.wait_ge(small_lo, 2)
                    gp.dma_start(wdt[:, :], w_dt[l]).then_inc(small_raw1, 16)
                gp.wait_ge(params_in, 64)
                gp.wait_ge(sb_z, 4 * l + 4)
                for c in range(2):
                    gp.wait_ge(dt_a, l + 1)
                    if c == 1:
                        gp.wait_ge(seg, 2 * l + 1)
                    gp.tensor_tensor(out=atri, in0=tri_le[:, :].unsqueeze(1).to_broadcast([P, HEADS, P]),
                                     in1=sdt[:, 3, c, :].unsqueeze(2).to_broadcast([P, HEADS, P]),
                                     op=ALU.mult).then_inc(a_tri, 1)
                    if c == 0:
                        gp.wait_ge(x_tok, 4 * l + 4)
                        gp.wait_ge(turned, 4 * (l * NNORM + N_MIX + 1))
                        for t in range(NT):
                            gp.tensor_tensor(out=xn[:, t, :].rearrange("p (h d) -> p h d", h=HEADS),
                                             in0=xtok[:, t, :].rearrange("p (h d) -> p h d", h=HEADS),
                                             in1=rowof(l, 2).unsqueeze(2).to_broadcast([P, HEADS, HD]),
                                             op=ALU.mult).then_inc(y_skip, 1)
                gp.wait_ge(y_skip, 2 * l + 2)
                gp.dma_start(xtok[:, :, :], mem.rearrange("(t p) d -> p t d", p=P)).then_inc(mem_in, 16)
                root(l * NNORM + N_SSD, 4, D // 2)
                root(l * NNORM + N_MEM, 2, D)
                root(l * NNORM + N_XA, 2, D)
                root(l * NNORM + N_FFN, 2, D)
            gp.wait_ge(xs_ps, 4 * DEPTH)
            gp.dma_start(grow, ffn_row.partition_broadcast(P)).then_inc(grow_in, 16)
            gp.dma_start(frow, final_row.partition_broadcast(P)).then_inc(frow_in, 16)
            root(DEPTH * NNORM, 2, D)

        @block.scalar
        def _(act):
            link = chain(act, act_chain)
            made = [0]

            def split(u):
                act.wait_ge(landed[u % NSEM], 16 * (u // NSEM + 1))
                if u >= HL:
                    act.wait_ge(unit_used, u - HL + 1)
                act.activation(whi[:, u % HL, :], raw[:, slot_of(u), :], ACT.Copy).then_inc(hi_made, 1)

            def feed(upto):
                for u in range(made[0], min(upto, MOE0 - 1) + 1):
                    split(u)
                made[0] = max(made[0], min(upto, MOE0 - 1) + 1)

            def result(l, name, j, part=0):
                u = UNIT_OF[l, name, j]
                feed(u + 2)
                act.wait_ge(unit_used, u + 1)
                return ps[:, OUT_NO[l, name, j, part] % 2, :]

            def squares(l, n, src):
                i = l * NNORM + n
                act.wait_ge(turned, 4 * i)
                for t in range(NT):
                    act.activation(xn[:, t, :], src[:, t, :], ACT.Square,
                                   accum_out=ss[:, 4 * i + t:4 * i + t + 1]).then_inc(sumsq, 1)

            def turn_hi(l, n, dst):
                i = l * NNORM + n
                for r in range(4):
                    act.wait_ge(turned, 4 * i + r + 1)
                    for k in range(2):
                        act.activation(dst[:, 2 * r + k, :], ps[:, 2 + r, k * S:(k + 1) * S], ACT.Copy,
                                       scale=gcol(l, n, 2 * r + k)).then_inc(turned_hi, 1)

            feed(1)
            act.wait_ge(params_in, 64)
            act.activation(wr_hi[:, :], wr[:, :], ACT.Copy).then_inc(small_hi, 1)
            for l in range(DEPTH):
                if l == 0:
                    act.wait_ge(h_in, 16)
                else:
                    act.wait_ge(h_ffn, 4 * l)
                squares(l, N_MIX, h)
                act.wait_ge(small_raw1 if l else small_raw, 16)
                act.activation(wdt_hi[:, :], wdt[:, :], ACT.Copy).then_inc(small_hi, 1)
                act.activation(sdt[:, 4, 0, :], rowof(l, 1), ACT.Exp).then_inc(small_hi, 1)
                turn_hi(l, N_MIX, u_hi)
                feed(UNIT_OF[l, "q", 0] + 2)
                act.wait_ge(dt_sum, l + 1)
                link(act.activation(sdt[:, 1, :, :], sdt[:, 0, :, :], ACT.Abs))
                link(act.activation(sdt[:, 1, :, :], sdt[:, 1, :, :], ACT.Exp, scale=-1.0))
                act.activation(sdt[:, 1, :, :], sdt[:, 1, :, :], ACT.Ln, bias=1.0).then_inc(dt_ln, 1)
                for n, j in [("q", 0), ("q", 1), ("k", 0), ("k", 1)]:
                    o = result(l, n, j)
                    c = (0 if n == "q" else 4) + 2 * j
                    act.activation(qk[:, c:c + 2, :], o.rearrange("p (a b) -> p a b", a=2), ACT.Copy,
                                   scale=(HD ** -0.5 if n == "q" else 1.0)).then_inc(out_read_act, 1)
                for j in range(2):
                    o = result(l, "v", j)
                    act.activation(va[:, :, 256 * j:256 * j + 256], o.rearrange("p (a b) -> p a b", a=2),
                                   ACT.Copy).then_inc(out_read_act, 1)
                act.wait_ge(dt_cum, l + 1)
                act.activation(eacum[:, :, :], ps[:, 7, 64:96].rearrange("p (a b) -> p a b", a=2),
                               ACT.Exp).then_inc(dt_exp, 1)

                def softplus_tail(p):
                    z = ps[:, 2 + 2 * (p % 2):4 + 2 * (p % 2), 0:384]
                    act.wait_ge(sb_z, 4 * l + p + 1)
                    if 4 * l + p >= 1:
                        act.wait_ge(sb_sp, 4 * l + p)
                    link(act.activation(sbl[:, :, :], z, ACT.Abs))
                    link(act.activation(sbl[:, :, :], sbl[:, :, :], ACT.Exp, scale=-1.0))
                    act.activation(sbl[:, :, :], sbl[:, :, :], ACT.Ln, bias=1.0).then_inc(sb_ln, 1)

                def exp_att(p):
                    act.wait_ge(sb_lp, 4 * l + p + 1)
                    if 4 * l + p >= 1:
                        act.wait_ge(sb_y, 4 * l + p)
                    act.activation(sba[:, :, :], ps[:, 2 + 2 * (p % 2):4 + 2 * (p % 2), 0:384],
                                   ACT.Exp).then_inc(sb_exp, 1)

                def y_out(p):
                    act.wait_ge(sb_y, 4 * l + p + 1)
                    act.activation(o_hi[:, p, :], ps[:, 6 + p % 2, 0:S], ACT.Copy).then_inc(sb_hi, 1)

                def pad(n):
                    j = (4, 0, 1, 2, 3)[n]
                    o = result(l, "xbc", j)
                    if l and n == 0:
                        act.wait_ge(merged_hi, 4 * l)
                        act.wait_ge(merged_lo, 4 * l)
                    act.activation(xconv[:, 2 * j:2 * j + 2, CONV - 1:], o.rearrange("p (a b) -> p a b", a=2),
                                   ACT.Copy).then_inc(out_read_act, 1)

                softplus_tail(0)
                softplus_tail(1)
                pad(0)
                exp_att(0)
                pad(1)
                softplus_tail(2)
                exp_att(1)
                y_out(0)
                pad(2)
                softplus_tail(3)
                exp_att(2)
                y_out(1)
                pad(3)
                exp_att(3)
                y_out(2)
                pad(4)
                y_out(3)
                for n, j in enumerate((4, 0, 1, 2, 3)):
                    act.wait_ge(conved, 5 * l + n + 1)
                    act.activation(xc[:, 2 * j:2 * j + 2, :], xc[:, 2 * j:2 * j + 2, :],
                                   ACT.Silu).then_inc(silued, 1)

                def gate(name, j):
                    o = result(l, name, j)
                    if name == "gb" and j < 2:
                        act.wait_ge(st_ps, l + 1)
                    if name == "gb" and j >= 2:
                        act.wait_ge(y_read, 2 * l + 2)
                    act.activation((ga if name == "ga" else gb)[:, 2 * j:2 * j + 2, :],
                                   o.rearrange("p (a b) -> p a b", a=2), ACT.Tanh,
                                   scale=0.5).then_inc(out_read_act, 1)

                def decays(c):
                    act.wait_ge(seg, 2 * l + c + 1)
                    if c == 1:
                        act.wait_ge(y_ps, 2 * l + 1)
                    act.activation(decay, ps[:, 2:6, :].rearrange("p a (b t) -> p (a b) t", t=P),
                                   ACT.Exp).then_inc(decayed, 1)

                act.wait_ge(sb_y, 4 * l + 4)
                gate("ga", 0)
                act.wait_ge(b_turned, l + 1)
                act.activation(btok[:, :], ps[:, 6, 0:P], ACT.Copy).then_inc(b_tok, 1)
                if l:
                    act.wait_ge(normed, 2 * ((l - 1) * NNORM + N_MEM + 1))
                for r in range(4):
                    act.wait_ge(x_turned, 4 * l + r + 1)
                    act.activation(xtok[:, r // 2, (r % 2) * 512:(r % 2) * 512 + 512], ps[:, 2 + r, :],
                                   ACT.Copy).then_inc(x_tok, 1)
                gate("ga", 1)
                decays(0)
                gate("ga", 2)
                act.wait_ge(st_ps, l + 1)
                act.activation(prev, ps[:, 2, :], ACT.Copy).then_inc(st_out, 1)
                gate("ga", 3)
                gate("gb", 0)
                decays(1)
                for j in range(1, 4):
                    gate("gb", j)
                for j in range(4):
                    o = result(l, "z", j)
                    if 4 * l + j >= 2:
                        act.wait_ge(z_mul, 4 * l + j - 1)
                    act.activation(zs[:, j % 2, :, :], o.rearrange("p (a b) -> p a b", a=2),
                                   ACT.Silu).then_inc(out_read_act, 1)
                i = l * NNORM + N_SSD
                act.wait_ge(z_mul, 4 * l + 4)
                for t in range(NT):
                    for g in range(2):
                        act.activation(merged[:, 4 * t + 2 * g:4 * t + 2 * g + 2, :], xn[:, t, 512 * g:512 * g + 512], ACT.Square,
                                       accum_out=ss[:, 4 * i + 2 * t + g:4 * i + 2 * t + g + 1]).then_inc(sumsq, 1)
                feed(UNIT_OF[l, "sbo", 0] + 2)
                turn_hi(l, N_SSD, m_hi)
                act.wait_ge(mem_in, 16 * (l + 1))
                squares(l, N_MEM, xtok)
                for j in range(4):
                    feed(UNIT_OF[l, "ssdo", j] + 2)
                    act.wait_ge(merged_sum, 4 * l + j + 1)
                    act.activation(u_hi[:, 2 * j:2 * j + 2, :], merged[:, 2 * j:2 * j + 2, :], ACT.Copy,
                                   scale=0.5).then_inc(merged_hi, 1)
                turn_hi(l, N_MEM, m_hi)
                feed(UNIT_OF[l, "wout", 3] + 2)
                act.wait_ge(out_read_dve, out_reader(OUT_NO[l, "wout", 3, 0])[1])
                squares(l, N_XA, h)
                for j in range(2):
                    o = result(l, "xk", j)
                    act.activation(kx[:, 2 * j:2 * j + 2, :], o.rearrange("p (a b) -> p a b", a=2),
                                   ACT.Copy).then_inc(out_read_act, 1)
                for j in range(2):
                    o = result(l, "xv", j)
                    act.activation(vx[:, :, 256 * j:256 * j + 256], o.rearrange("p (a b) -> p a b", a=2),
                                   ACT.Copy).then_inc(out_read_act, 1)
                turn_hi(l, N_XA, u_hi)
                for j in range(2):
                    o = result(l, "xq", j)
                    act.activation(qx[:, 2 * j:2 * j + 2, :], o.rearrange("p (a b) -> p a b", a=2),
                                   ACT.Copy).then_inc(out_read_act, 1)
                for a in range(XH):
                    act.wait_ge(xs_max, 4 * l + a + 1)
                    for t in range(NT):
                        act.activation(prob[:, 2 * a + t, :], ps[:, 2 + a, t * S:(t + 1) * S], ACT.Exp,
                                       scale=XSCALE, bias=xmx[:, 1, a, t:t + 1],
                                       accum_out=xmx[:, 2, a, t:t + 1]).then_inc(xs_exp, 1)
                for a in range(XH):
                    act.wait_ge(xp_turned, 4 * l + a + 1)
                    if 4 * l + a >= 2:
                        act.wait_ge(xo_ps, 4 * l + a - 1)
                    act.activation(pT[:, 2 * (a % 2):2 * (a % 2) + 2, :],
                                   ps[:, 2 + a, :].rearrange("p (a b) -> p a b", a=2), ACT.Copy).then_inc(xp_out, 1)
                    if a >= 1:
                        act.wait_ge(xo_ps, 4 * l + a)
                        act.activation(o_hi[:, a - 1, :], ps[:, 6 + (a - 1) % 2, 0:S], ACT.Copy).then_inc(xo_hi, 1)
                act.wait_ge(xo_ps, 4 * l + 4)
                act.activation(o_hi[:, 3, :], ps[:, 7, 0:S], ACT.Copy).then_inc(xo_hi, 1)
                feed(UNIT_OF[l, "xo", 1] + 2)
                act.wait_ge(out_read_dve, out_reader(OUT_NO[l, "xo", 1, 1])[1])
                squares(l, N_FFN, h)
                turn_hi(l, N_FFN, u_hi)
                if l == 0:
                    for c in range(CH):
                        for f in range(2):
                            n = 2 * c + f
                            feed(FFN0 + up_unit(c) + 2)
                            if f == 0:
                                act.wait_ge(gu_ps, c + 1)
                            else:
                                act.wait_ge(unit_used, FFN0 + up_unit(c) + 1)
                            if n >= 2:
                                act.wait_ge(f_act, n - 1)
                            else:
                                act.wait_ge(out_read_dve, sum(o[0] == 0 and o[1] in BY_DVE for o in OUTS))
                            act.activation(sg[:, f, :], ps[:, n % 4, 0:S], ACT.Silu).then_inc(f_silu, 1)
                        if c >= 2:
                            act.wait_ge(unit_used, FFN0 + down_unit(c - 2) + 1)
                        for f in range(2):
                            act.wait_ge(f_act, 2 * c + f + 1)
                            act.activation(hT_hi[:, c % 2, f, :], act_f[:, f, :], ACT.Copy).then_inc(f_hi, 1)
                    feed(LAYER1 + 2)

            feed(MOE0 - 1)
            act.wait_ge(ut_made, 1)
            act.activation(mt_hi, xtok[:, :, :], ACT.Copy).then_inc(ut_hi, 1)
            act.wait_ge(r_mask, 1)
            act.activation(rt1[:, 4, :], rt1[:, 3, :], ACT.Exp).then_inc(r_exp, 1)
            act.wait_ge(r_done, 1)
            n_visits = act.value_load(visits_i[0:1, 0:1], min_val=NE, max_val=2 * NE)

            def gathered(count, r):
                act.wait_ge(ue_ps, count)
                act.activation(ue_hi[:, 4 * r:4 * r + 4, :], ps[:, 6 + r, :].rearrange("p (a b) -> p a b", a=4),
                               ACT.Copy).then_inc(ue_hi_out, 1)

            def y_half(used):
                act.wait_ge(unit_used, used)
                act.activation(y_hi, ps[:, 4:6, :].rearrange("p a b -> p (a b)"), ACT.Copy,
                               scale=wslot[:, 0:1]).then_inc(e_yhi, 1)

            for r in range(2):
                gathered(r + 1, r)
            with act.Fori(0, n_visits) as n:
                slots = [act.snap((n * EU + (RAW + s)) % RAW_E) for s in range(RAW_E)]

                def split_e(j):
                    act.wait_ge(landed[(MOE0 + j) % NSEM], n * (16 * EU // NSEM) + 16 * ((MOE0 + j) // NSEM + 1))
                    act.wait_ge(unit_used, n * EU + (MOE0 + j - HL + 1))
                    act.sem_inc(unit_begun, 1)
                    act.activation(whi[:, (MOE0 + j) % HL, :], raw_e[:, bass.ds(slots[j % RAW_E], 1), :],
                                   ACT.Copy).then_inc(hi_made, 1)

                for c in range(CH):
                    if c == 0:
                        split_e(0)
                        split_e(1)
                        y_half(n * EU + MOE0)
                        split_e(2)
                    else:
                        split_e(3 * c + 2)
                    act.wait_ge(unit_used, n * EU + (MOE0 + up_unit(c) + 1))
                    if c >= 2:
                        act.wait_ge(e_act, n * CH + (c - 1))
                    act.activation(sg[:, c % 2, :], ps[:, c % 2, 0:256], ACT.Silu).then_inc(e_silu, 1)
                    for j in range(3 * c + 3, min(3 * c + 4, EU - 1) + 1):
                        split_e(j)
                    if c == CH - 1:
                        for r in range(2):
                            gathered(2 * n + (r + 3), r)
                    act.wait_ge(e_turn, n * CH + (c + 1))
                    act.activation(hT_hi[:, c % 2, 0, :], ps[:, 2 + c % 2, 0:256], ACT.Copy).then_inc(e_hi, 1)
                    if c == 0:
                        act.wait_ge(selT_ps, n + 1)
                        act.activation(selT[:, :], ps[:, 6, 0:S], ACT.Copy).then_inc(selT_out, 1)
                        act.wait_ge(w_ps, n + 1)
                        act.activation(wslot[:, :], ps[:, 7, 0:1], ACT.Copy).then_inc(w_out_s, 1)
            y_half(n_visits * EU + MOE0)
            i = DEPTH * NNORM
            for t in range(NT):
                act.wait_ge(e_add, n_visits * 4 + (2 * t + 3))
                act.activation(xn[:, t, :], h[:, t, :], ACT.Square,
                               accum_out=ss[:, 4 * i + t:4 * i + t + 1]).then_inc(sumsq, 1)

        @block.vector
        def _(dve):
            link = chain(dve, dve_chain)
            made = [0]

            def split(u):
                dve.wait_ge(hi_made, u + 1)
                dve.tensor_tensor(out=wlo[:, u % HL, :], in0=raw[:, slot_of(u), :],
                                  in1=whi[:, u % HL, :].bitcast(F32), op=ALU.subtract).then_inc(lo_made, 1)

            def feed(upto):
                for u in range(made[0], min(upto, MOE0 - 1) + 1):
                    split(u)
                made[0] = max(made[0], min(upto, MOE0 - 1) + 1)

            def result(l, name, j, part=0):
                u = UNIT_OF[l, name, j]
                feed(u + 2)
                dve.wait_ge(unit_used, u + 1)
                return ps[:, OUT_NO[l, name, j, part] % 2, :]

            def normalise(l, n, src):
                i = l * NNORM + n
                dve.wait_ge(rstd, i + 1)
                for t in range(NT):
                    dve.tensor_scalar(xn[:, t, :], src[:, t, :], rs[:, 4 * i + t:4 * i + t + 1], None,
                                      ALU.mult).then_inc(normed, 1)

            def turn_lo(l, n, hi, lo):
                i = l * NNORM + n
                for r in range(4):
                    dve.wait_ge(turned_hi, 8 * i + 2 * r + 2)
                    for k in range(2):
                        dve.scalar_tensor_tensor(lo[:, 2 * r + k, :], ps[:, 2 + r, k * S:(k + 1) * S],
                                                 gcol(l, n, 2 * r + k), hi[:, 2 * r + k, :].bitcast(F32),
                                                 ALU.mult, ALU.subtract).then_inc(turned_lo, 1)

            feed(1)
            dve.wait_ge(small_hi, 1)
            dve.tensor_tensor(out=wr_lo[:, :], in0=wr[:, :], in1=wr_hi[:, :].bitcast(F32),
                              op=ALU.subtract).then_inc(small_lo, 1)
            for l in range(DEPTH):
                if l == 0:
                    dve.wait_ge(h_in, 16)
                normalise(l, N_MIX, h)
                dve.wait_ge(small_hi, 2 * l + 3)
                dve.tensor_tensor(out=wdt_lo[:, :], in0=wdt[:, :], in1=wdt_hi[:, :].bitcast(F32),
                                  op=ALU.subtract).then_inc(small_lo, 1)
                turn_lo(l, N_MIX, u_hi, u_lo)
                feed(UNIT_OF[l, "q", 0] + 2)
                dve.wait_ge(dt_ps, l + 1)
                link(dve.tensor_tensor(out=sdt[:, 0, :, :], in0=ps[:, 7, 0:32].rearrange("p (a b) -> p a b", a=2),
                                       in1=rowof(l, 0).unsqueeze(1).to_broadcast([P, NT, HEADS]), op=ALU.add))
                dve.tensor_scalar(sdt[:, 5, :, :], sdt[:, 0, :, :], 0.0, None, ALU.max).then_inc(dt_sum, 1)
                dve.wait_ge(dt_ln, l + 1)
                link(dve.tensor_tensor(out=sdt[:, 2, :, :], in0=sdt[:, 5, :, :], in1=sdt[:, 1, :, :], op=ALU.add))
                dve.scalar_tensor_tensor(sdt[:, 3, :, :], sdt[:, 2, :, :], -1.0,
                                         sdt[:, 4, 0, :].unsqueeze(1).to_broadcast([P, NT, HEADS]),
                                         ALU.mult, ALU.mult).then_inc(dt_a, 1)

                def blocks(t):
                    return t[:, :, :].rearrange("p h (b c) -> p h b c", b=3)[:, :, 0:3:2, :]

                def softplus(p):
                    z = ps[:, 2 + 2 * (p % 2):4 + 2 * (p % 2), 0:384]
                    dve.wait_ge(sb_ln, 4 * l + p + 1)
                    if 4 * l + p >= 1:
                        dve.wait_ge(sb_lp, 4 * l + p)
                    link(dve.scalar_tensor_tensor(sbp[:, :, :], z, 0.0, sbl[:, :, :], ALU.max, ALU.add))
                    dve.tensor_tensor(out=blocks(sbp), in0=blocks(sbp),
                                      in1=tri_lt[:, :].unsqueeze(1).unsqueeze(1).to_broadcast([P, 2, 2, P]),
                                      op=ALU.mult).then_inc(sb_sp, 1)

                def mask_att(p):
                    dve.wait_ge(sb_exp, 4 * l + p + 1)
                    for a in range(2):
                        b = blocks(sba)[:, a]
                        dve.scalar_tensor_tensor(b, b, 1.0, tri_lt[:, :].unsqueeze(1).to_broadcast([P, 2, P]),
                                                 ALU.min, ALU.mult).then_inc(sb_att, 1)

                def y_lo_out(p):
                    dve.wait_ge(sb_hi, 4 * l + p + 1)
                    dve.tensor_tensor(out=o_lo[:, p, :], in0=ps[:, 6 + p % 2, 0:S],
                                      in1=o_hi[:, p, :].bitcast(F32), op=ALU.subtract).then_inc(sb_lo, 1)

                def conv(n):
                    j = (4, 0, 1, 2, 3)[n]
                    if l == 0 and n == 0:
                        dve.wait_ge(params_in, 64)
                    if n == 0:
                        if l:
                            dve.wait_ge(merged_hi, 4 * l)
                            dve.wait_ge(xs_ps, 4 * l)
                        link(dve.memset(xconv[:, :, 0:CONV - 1], 0.0))
                    feed(UNIT_OF[l, "xbc", j] + 2)
                    dve.wait_ge(out_read_act, out_reader(OUT_NO[l, "xbc", j, 0])[1])
                    for i in range(CONV):
                        for f in (2 * j, 2 * j + 1):
                            w0 = (l * CT + f) * (CONV + 1)
                            src = xconv[:, f, i:i + S]
                            if i == 0:
                                ins = dve.tensor_scalar(xc[:, f, :], src, cw[:, w0:w0 + 1],
                                                        cw[:, w0 + CONV:w0 + CONV + 1], ALU.mult, ALU.add)
                            else:
                                ins = dve.scalar_tensor_tensor(xc[:, f, :], src, cw[:, w0 + i:w0 + i + 1],
                                                               xc[:, f, :], ALU.mult, ALU.add)
                        if i < CONV - 1:
                            link(ins)
                        else:
                            ins.then_inc(conved, 1)

                feed(UNIT_OF[l, "v", 1] + 2)
                softplus(0)
                softplus(1)
                conv(0)
                mask_att(0)
                conv(1)
                softplus(2)
                mask_att(1)
                y_lo_out(0)
                conv(2)
                softplus(3)
                mask_att(2)
                y_lo_out(1)
                conv(3)
                mask_att(3)
                y_lo_out(2)
                conv(4)
                y_lo_out(3)
                feed(UNIT_OF[l, "ga", 0] + 2)
                dve.wait_ge(b_tok, l + 1)
                for g in range(2):
                    dve.tensor_tensor(out=cbm[:, :, g, :], in0=ps[:, 7 - g, P:3 * P].rearrange("p (a c) -> p a c", a=2),
                                      in1=tri_le[:, :].unsqueeze(1).to_broadcast([P, 2, P]),
                                      op=ALU.mult).then_inc(cb_made, 1)
                for r in range(4):
                    t, g = r // 2, r % 2
                    dve.wait_ge(x_tok, 4 * l + r + 1)
                    dve.tensor_tensor(out=xdt[:, t, 512 * g:512 * g + 512].rearrange("p (h d) -> p h d", h=8),
                                      in0=ps[:, 2 + r, :].rearrange("p (h d) -> p h d", h=8),
                                      in1=sdt[:, 2, t, 8 * g:8 * g + 8].unsqueeze(2).to_broadcast([P, 8, HD]),
                                      op=ALU.mult).then_inc(x_dt, 1)
                dve.wait_ge(dt_exp, l + 1)
                dve.wait_ge(x_dt, 4 * l + 2)
                if l:
                    dve.wait_ge(xp_turned, 4 * l)
                dve.tensor_tensor(out=xdte.rearrange("p (h d) -> p h d", h=HEADS),
                                  in0=xdt[:, 0, :].rearrange("p (h d) -> p h d", h=HEADS),
                                  in1=eacum[:, 1, :].unsqueeze(2).to_broadcast([P, HEADS, HD]),
                                  op=ALU.mult).then_inc(st_in, 1)

                def head_products(c):
                    dve.wait_ge(cb_made, 2 * l + 2)
                    dve.wait_ge(decayed, 2 * l + c + 1)
                    for g in range(2):
                        d = decay[:, 8 * g:8 * g + 8, :]
                        dve.tensor_tensor(out=d, in0=d, in1=cbm[:, c, g, :].unsqueeze(1).to_broadcast([P, 8, P]),
                                          op=ALU.mult).then_inc(m_made, 1)

                def add_y(c):
                    dve.wait_ge(y_skip, 2 * l + c + 1)
                    dve.wait_ge(y_ps, 2 * l + c + 1)
                    dve.tensor_tensor(out=xn[:, c, :], in0=xn[:, c, :],
                                      in1=ps[:, 6:8, :].rearrange("p a b -> p (a b)"), op=ALU.add).then_inc(y_read, 1)

                feed(UNIT_OF[l, "ga", 1] + 2)
                head_products(0)
                feed(UNIT_OF[l, "ga", 3] + 2)
                add_y(0)
                dve.wait_ge(yoff_ps, l + 1)
                for g in range(2):
                    dve.tensor_tensor(out=yoff[:, 512 * g:512 * g + 512].rearrange("p (h d) -> p h d", h=8),
                                      in0=ps[:, 2 + g, :].rearrange("p (h d) -> p h d", h=8),
                                      in1=eacum[:, 0, 8 * g:8 * g + 8].unsqueeze(2).to_broadcast([P, 8, HD]),
                                      op=ALU.mult).then_inc(yoff_read, 1)
                feed(UNIT_OF[l, "gb", 0] + 2)
                dve.wait_ge(yoff_read, 2 * l + 2)
                dve.wait_ge(y_skip, 2 * l + 2)
                dve.tensor_tensor(out=xn[:, 1, :], in0=xn[:, 1, :], in1=yoff, op=ALU.add).then_inc(yoff_added, 1)
                head_products(1)
                feed(UNIT_OF[l, "gb", 1] + 2)
                dve.wait_ge(yoff_added, l + 1)
                add_y(1)
                for j in range(4):
                    feed(UNIT_OF[l, "z", j] + 2)
                    dve.wait_ge(out_read_act, out_reader(OUT_NO[l, "z", j, 0])[1])
                    dve.wait_ge(y_read, 2 * l + 2)
                    dve.tensor_tensor(out=xn[:, :, 256 * j:256 * j + 256], in0=xn[:, :, 256 * j:256 * j + 256],
                                      in1=zs[:, j % 2, :, :], op=ALU.mult).then_inc(z_mul, 1)
                feed(UNIT_OF[l, "sbo", 0] + 2)
                i = l * NNORM + N_SSD
                dve.wait_ge(rstd, i + 1)
                for t in range(NT):
                    dve.tensor_tensor(out=xn[:, t, :].rearrange("p (g f) -> p g f", g=2),
                                      in0=xn[:, t, :].rearrange("p (g f) -> p g f", g=2),
                                      in1=rs[:, 4 * i + 2 * t:4 * i + 2 * t + 2].unsqueeze(2)
                                      .to_broadcast([P, 2, D // 2]), op=ALU.mult).then_inc(normed, 1)
                turn_lo(l, N_SSD, m_hi, m_lo)
                normalise(l, N_MEM, xtok)
                for j in range(2):
                    for part in range(2):
                        o = result(l, "sbo", j, part)
                        f = 4 * j + 2 * part
                        dve.scalar_tensor_tensor(merged[:, f:f + 2, :], gb[:, f:f + 2, :], 1.0,
                                                 o.rearrange("p (a b) -> p a b", a=2), ALU.add,
                                                 ALU.mult).then_inc(out_read_dve, 1)

                def merged_lo_half(j):
                    dve.wait_ge(merged_hi, 4 * l + j + 1)
                    dve.scalar_tensor_tensor(u_lo[:, 2 * j:2 * j + 2, :], merged[:, 2 * j:2 * j + 2, :], 0.5,
                                             u_hi[:, 2 * j:2 * j + 2, :].bitcast(F32), ALU.mult,
                                             ALU.subtract).then_inc(merged_lo, 1)

                for j in range(4):
                    o = result(l, "ssdo", j)
                    part = zs[:, 0, :, :]
                    if j == 0:
                        dve.wait_ge(z_mul, 4 * l + 4)
                    else:
                        dve.wait_ge(merged_sum, 4 * l + j)
                    dve.scalar_tensor_tensor(part, ga[:, 2 * j:2 * j + 2, :], 1.0,
                                             o.rearrange("p (a b) -> p a b", a=2), ALU.add,
                                             ALU.mult).then_inc(out_read_dve, 1)
                    dve.wait_ge(out_read_dve, out_reader(OUT_NO[l, "ssdo", j, 0])[1])
                    dve.tensor_tensor(out=merged[:, 2 * j:2 * j + 2, :], in0=merged[:, 2 * j:2 * j + 2, :],
                                      in1=part, op=ALU.add).then_inc(merged_sum, 1)
                    if j:
                        merged_lo_half(j - 1)
                merged_lo_half(3)
                turn_lo(l, N_MEM, m_hi, m_lo)
                for j in range(4):
                    o = result(l, "wout", j)
                    dve.tensor_tensor(out=h[:, :, 256 * j:256 * j + 256], in0=h[:, :, 256 * j:256 * j + 256],
                                      in1=o.rearrange("p (a b) -> p a b", a=2), op=ALU.add)\
                        .then_inc(out_read_dve, 1)
                feed(UNIT_OF[l, "xk", 0] + 2)
                normalise(l, N_XA, h)
                feed(UNIT_OF[l, "xv", 1] + 2)
                turn_lo(l, N_XA, u_hi, u_lo)
                feed(UNIT_OF[l, "xq", 1] + 2)
                for a in range(XH):
                    dve.wait_ge(xs_ps, 4 * l + a + 1)
                    link(dve.tensor_reduce(xmx[:, 0, a, :], ps[:, 2 + a, :].rearrange("p (t m) -> p t m", t=NT),
                                           AX.X, ALU.max))
                    dve.tensor_scalar(xmx[:, 1, a, :], xmx[:, 0, a, :], -XSCALE, None, ALU.mult).then_inc(xs_max, 1)
                for a in range(XH):
                    dve.wait_ge(xs_exp, 8 * l + 2 * a + 2)
                    link(dve.reciprocal(xmx[:, 3, a, :], xmx[:, 2, a, :]))
                    for t in range(NT):
                        dve.tensor_scalar(prob[:, 2 * a + t, :], prob[:, 2 * a + t, :], xmx[:, 3, a, t:t + 1], None,
                                          ALU.mult).then_inc(xs_p, 1)
                for a in range(XH):
                    dve.wait_ge(xo_hi, 4 * l + a + 1)
                    dve.tensor_tensor(out=o_lo[:, a, :], in0=ps[:, 6 + a % 2, 0:S],
                                      in1=o_hi[:, a, :].bitcast(F32), op=ALU.subtract).then_inc(xo_lo, 1)
                for j in range(2):
                    for part in range(2):
                        o = result(l, "xo", j, part)
                        dve.tensor_tensor(out=h[:, part, 512 * j:512 * j + 512], in0=h[:, part, 512 * j:512 * j + 512],
                                          in1=o, op=ALU.add).then_inc(out_read_dve, 1)
                normalise(l, N_FFN, h)
                turn_lo(l, N_FFN, u_hi, u_lo)
                if l == 0:
                    for c in range(CH):
                        for f in range(2):
                            n = 2 * c + f
                            feed(FFN0 + up_unit(c) + 2)
                            if n >= 2:
                                dve.wait_ge(f_hi, n - 1)
                                dve.wait_ge(f_lo, n - 1)
                            dve.wait_ge(f_silu, n + 1)
                            dve.tensor_tensor(out=act_f[:, f, :], in0=sg[:, f, :], in1=ps[:, n % 4, S:2 * S],
                                              op=ALU.mult).then_inc(f_act, 1)
                        for f in range(2):
                            dve.wait_ge(f_hi, 2 * c + f + 1)
                            dve.tensor_tensor(out=hT_lo[:, c % 2, f, :], in0=act_f[:, f, :],
                                              in1=hT_hi[:, c % 2, f, :].bitcast(F32), op=ALU.subtract).then_inc(f_lo, 1)
                    feed(LAYER1 + 2)
                    dve.wait_ge(unit_used, LAYER1)
                    for t in range(NT):
                        for a in range(2):
                            dve.tensor_tensor(out=h[:, t, 512 * a:512 * a + 512], in0=h[:, t, 512 * a:512 * a + 512],
                                              in1=ps[:, 4 + 2 * t + a, :], op=ALU.add).then_inc(h_ffn, 1)

            def select(column):
                for t in range(NT):
                    dve.tensor_scalar(sel[:, t, :], iota[:, :], rank2[:, t, column],
                                      mask2[:, t, column], ALU.is_equal, ALU.mult).then_inc(sel_made, 1)

            feed(MOE0 - 1)
            dve.memset(selT[:, :].bitcast(F32), 0.0)
            dve.memset(wslot[:, :], 0.0)
            for v in (rank2, mask2, comb2):
                link(dve.memset(v[:, :, 2 * NE:], 0.0))
            dve.wait_ge(grow_in, 16)
            dve.tensor_tensor(out=xtok[:, :, :], in0=xn[:, :, :], in1=grow.unsqueeze(1).to_broadcast([P, NT, D]),
                              op=ALU.mult).then_inc(ut_made, 1)
            dve.wait_ge(consts, 10)
            dve.wait_ge(r_ps, 1)
            logit, left, eq, best, one0, one1, mask, rank = (rt[:, i] for i in range(8))
            frst = first[:, :].unsqueeze(1).to_broadcast([P, NT, NE])

            def wide(v):
                return v.unsqueeze(2).to_broadcast([P, NT, NE])

            link(dve.tensor_copy(logit, ps[:, 6, 0:NT * NE].rearrange("p (t e) -> p t e", t=NT)))
            link(dve.tensor_copy(left, logit))
            for i, one in enumerate((one0, one1)):
                link(dve.tensor_reduce(rt1[:, i, :], left, AX.X, ALU.max))
                link(dve.tensor_tensor(out=eq, in0=left, in1=wide(rt1[:, i, :]), op=ALU.is_equal))
                link(dve.tensor_tensor(out=best, in0=eq, in1=frst, op=ALU.mult))
                link(dve.tensor_reduce(rt1[:, 2, :], best, AX.X, ALU.max))
                link(dve.tensor_tensor(out=one, in0=best, in1=wide(rt1[:, 2, :]), op=ALU.is_equal))
                if i == 0:
                    link(dve.scalar_tensor_tensor(left, one, -3.0e38, logit, ALU.mult, ALU.add))
            link(dve.tensor_tensor(out=rt1[:, 3, :], in0=rt1[:, 1, :], in1=rt1[:, 0, :], op=ALU.subtract))
            dve.tensor_tensor(out=mask, in0=one0, in1=one1, op=ALU.add).then_inc(r_mask, 1)
            dve.wait_ge(r_exp, 1)
            link(dve.tensor_scalar(rt1[:, 5, :], rt1[:, 4, :], 1.0, None, ALU.add))
            link(dve.reciprocal(rt1[:, 6, :], rt1[:, 5, :]))
            link(dve.tensor_tensor(out=rt1[:, 7, :], in0=rt1[:, 4, :], in1=rt1[:, 6, :], op=ALU.mult))
            link(dve.tensor_tensor(out=one0, in0=one0, in1=wide(rt1[:, 6, :]), op=ALU.mult))
            link(dve.tensor_tensor(out=one1, in0=one1, in1=wide(rt1[:, 7, :]), op=ALU.mult))
            for i in range(2):
                e = slice(NE * i, NE * i + NE)
                link(dve.tensor_tensor(out=comb2[:, :, e], in0=one0, in1=one1, op=ALU.add))
                link(dve.tensor_copy(mask2[:, :, e], mask))
            dve.wait_ge(r_rank, 1)
            link(dve.tensor_copy(rank2[:, :, 0:NE], ps[:, 7, 0:16].rearrange("p (t e) -> p t e", t=NT)))
            link(dve.tensor_scalar(rank2[:, :, NE:2 * NE], rank2[:, :, 0:NE], -128.0, None, ALU.add))
            link(dve.tensor_reduce(visits[:, 0:1], ps[:, 7, 16:24], AX.X, ALU.max))
            link(dve.tensor_scalar(visits[:, 1:2], visits[:, 0:1], 128.5, float(NE), ALU.is_gt, ALU.mult))
            link(dve.tensor_scalar(visits[:, 2:3], visits[:, 1:2], float(NE), None, ALU.add))
            dve.tensor_copy(visits_i[:, :], visits[:, 2:3]).then_inc(r_done, 1)
            select(slice(0, 1))
            dve.wait_ge(ut_hi, 1)
            dve.tensor_tensor(out=mt_lo, in0=xtok[:, :, :], in1=mt_hi.bitcast(F32), op=ALU.subtract)\
                .then_inc(e_add, 1)
            dve.wait_ge(r_done, 1)
            n_visits = dve.value_load(visits_i[0:1, 0:1], min_val=NE, max_val=2 * NE)

            def gathered(count, r):
                dve.wait_ge(ue_hi_out, count)
                dve.tensor_tensor(out=ue_lo[:, 4 * r:4 * r + 4, :],
                                  in0=ps[:, 6 + r, :].rearrange("p (a b) -> p a b", a=4),
                                  in1=ue_hi[:, 4 * r:4 * r + 4, :].bitcast(F32),
                                  op=ALU.subtract).then_inc(ue_lo_out, 1)

            def y_half(count):
                dve.wait_ge(e_yhi, count)
                dve.scalar_tensor_tensor(y_lo, ps[:, 4:6, :].rearrange("p a b -> p (a b)"), wslot[:, 0:1],
                                         y_hi.bitcast(F32), ALU.mult, ALU.subtract).then_inc(e_ylo, 1)

            def add_y(count, i):
                dve.wait_ge(e_sc, count)
                c = slice(512 * (i % 2), 512 * (i % 2) + 512)
                dve.tensor_tensor(out=h[:, i // 2, c], in0=h[:, i // 2, c], in1=ps[:, 6 + i % 2, :],
                                  op=ALU.add).then_inc(e_add, 1)

            for r in range(2):
                gathered(r + 1, r)
            with dve.Fori(0, n_visits) as n:
                slots = [dve.snap((n * EU + (RAW + s)) % RAW_E) for s in range(RAW_E)]

                def split_e(j):
                    dve.wait_ge(hi_made, n * EU + (MOE0 + j + 1))
                    dve.tensor_tensor(out=wlo[:, (MOE0 + j) % HL, :], in0=raw_e[:, bass.ds(slots[j % RAW_E], 1), :],
                                      in1=whi[:, (MOE0 + j) % HL, :].bitcast(F32),
                                      op=ALU.subtract).then_inc(lo_made, 1)

                for c in range(CH):
                    if c == 0:
                        split_e(0)
                        split_e(1)
                        y_half(n + 1)
                        split_e(2)
                    else:
                        split_e(3 * c + 2)
                    dve.wait_ge(e_silu, n * CH + (c + 1))
                    if c >= 2:
                        dve.wait_ge(e_turn, n * CH + (c - 1))
                    dve.tensor_tensor(out=act_f[:, c % 2, :], in0=sg[:, c % 2, :], in1=ps[:, c % 2, 256:512],
                                      op=ALU.mult).then_inc(e_act, 1)
                    if c == 0:
                        add_y(n * 4 + 1, 0)
                        add_y(n * 4 + 2, 1)
                    for j in range(3 * c + 3, min(3 * c + 4, EU - 1) + 1):
                        split_e(j)
                    if c == CH - 1:
                        for r in range(2):
                            gathered(2 * n + (r + 3), r)
                    dve.wait_ge(e_hi, n * CH + (c + 1))
                    dve.tensor_tensor(out=hT_lo[:, c % 2, 0, :], in0=ps[:, 2 + c % 2, 0:256],
                                      in1=hT_hi[:, c % 2, 0, :].bitcast(F32), op=ALU.subtract).then_inc(e_lo, 1)
                    if c == 0:
                        add_y(n * 4 + 3, 2)
                        add_y(n * 4 + 4, 3)
                    if c == 2:
                        dve.wait_ge(w_ps, n + 1)
                        select(bass.ds(n + 1, 1))
            y_half(n_visits + 1)
            for i in range(4):
                add_y(n_visits * 4 + (i + 1), i)
            i = DEPTH * NNORM
            dve.wait_ge(rstd, i + 1)
            dve.wait_ge(frow_in, 16)
            for t in range(NT):
                dve.scalar_tensor_tensor(xn[:, t, :], h[:, t, :], rs[:, 4 * i + t:4 * i + t + 1], frow,
                                         ALU.mult, ALU.mult).then_inc(final_made, 1)

        @block.tensor
        def _(pe):
            def three(o, a_hi, a_lo, b_hi, b_lo, start, stop):
                pe.matmul(o, a_hi, b_hi, start=start, stop=False)
                pe.matmul(o, a_lo, b_hi, start=False, stop=False)
                return pe.matmul(o, a_hi, b_lo, start=False, stop=stop)

            def w(buf, u, k, c, n, width):
                return buf[:, u % HL, k * width + c:k * width + c + n]

            def begin(l, name, j, part=0):
                i = OUT_NO[l, name, j, part]
                if part == 0:
                    pe.wait_ge(lo_made, UNIT_OF[l, name, j] + 1)
                if i >= 2:
                    dve, count = out_reader(i - 2)
                    pe.wait_ge(out_read_dve if dve else out_read_act, count)
                return ps[:, i % 2, :]

            def by_token(l, name, j, a_hi, a_lo):
                u, o = UNIT_OF[l, name, j], begin(l, name, j)
                for t in range(NT):
                    for k in range(KD):
                        ins = three(o[:, 256 * t:256 * t + 256], a_hi[:, k, P * t:P * t + P], a_lo[:, k, P * t:P * t + P],
                                    w(whi, u, k, 0, 256, 256), w(wlo, u, k, 0, 256, 256), k == 0, k == KD - 1)
                ins.then_inc(unit_used, 1)

            def by_feature(l, name, j, a_hi, a_lo):
                u, o = UNIT_OF[l, name, j], begin(l, name, j)
                for f in range(2):
                    for k in range(KD):
                        ins = three(o[:, S * f:S * f + S], w(whi, u, k, P * f, P, 256), w(wlo, u, k, P * f, P, 256),
                                    a_hi[:, k, :], a_lo[:, k, :], k == 0, k == KD - 1)
                ins.then_inc(unit_used, 1)

            def turn(l, n, free_sem, free):
                i = l * NNORM + n
                pe.wait_ge(normed, 2 * i + 2)
                pe.wait_ge(free_sem, free)
                for r in range(4):
                    for k in range(2):
                        for t in range(NT):
                            f = 2 * r + k
                            ins = pe.transpose(ps[:, 2 + r, S * k + P * t:S * k + P * t + P],
                                               xn[:, t, P * f:P * f + P], ident[:, :])
                    ins.then_inc(turned, 1)

            def turned_ready(l, n):
                i = l * NNORM + n
                pe.wait_ge(turned_hi, 8 * (i + 1))
                pe.wait_ge(turned_lo, 8 * (i + 1))

            pe.wait_ge(consts, 10)
            for l in range(DEPTH):
                if l == 0:
                    turn(l, N_MIX, consts, 10)
                else:
                    turn(l, N_MIX, h_ffn, 4)
                turned_ready(l, N_MIX)
                pe.wait_ge(small_lo, l + 2)
                for t in range(NT):
                    for k in range(KD):
                        c = slice(16 * k, 16 * k + 16)
                        ins = three(ps[:, 7, 16 * t:16 * t + 16], u_hi[:, k, P * t:P * t + P], u_lo[:, k, P * t:P * t + P],
                                    wdt_hi[:, c], wdt_lo[:, c], k == 0, k == KD - 1)
                ins.then_inc(dt_ps, 1)
                for name, j in (("q", 0), ("q", 1), ("k", 0), ("k", 1)):
                    by_feature(l, name, j, u_hi, u_lo)
                pe.wait_ge(dt_a, l + 1)
                pe.matmul(ps[:, 7, 64:80], tri_le[:, :], sdt[:, 3, 1, :], start=True, stop=True)
                pe.matmul(ps[:, 7, 80:96], tri_gt[:, :], sdt[:, 3, 0, :], start=True, stop=True).then_inc(dt_cum, 1)
                for j in range(2):
                    by_token(l, "v", j, u_hi, u_lo)

                def scores(p):
                    pe.wait_ge(out_read_act, out_reader(OUT_NO[l, "k", 1, 0])[1])
                    if p >= 2:
                        pe.wait_ge(sb_exp, 4 * l + p - 1)
                    elif l == 0:
                        pe.wait_ge(turned_lo, 8)
                    for a in range(2):
                        o = ps[:, 2 + 2 * (p % 2) + a, :]
                        r = slice(HD * a, HD * a + HD)
                        pe.matmul(o[:, 0:S], qk[r, 4 + p, 0:P], qk[r, p, 0:S], start=True, stop=False,
                                  skip_group_check=True)
                        ins = pe.matmul(o[:, S:S + P], qk[r, 4 + p, P:S], qk[r, p, P:S], start=False, stop=False,
                                        skip_group_check=True)
                    ins.then_inc(sb_z, 1)

                def log_between(p):
                    pe.wait_ge(sb_sp, 4 * l + p + 1)
                    for a in range(2):
                        o = ps[:, 2 + 2 * (p % 2) + a, :]
                        pe.matmul(o[:, 0:S], neg_ge[:, :], sbp[:, a, 0:S], start=False, stop=False,
                                  skip_group_check=True)
                        pe.matmul(o[:, P:S], neg_one[:, :], sbp[:, a, S:S + P], start=False, stop=False,
                                  skip_group_check=True)
                        ins = pe.matmul(o[:, S:S + P], neg_ge[:, :], sbp[:, a, S:S + P], start=False, stop=True,
                                        skip_group_check=True)
                    ins.then_inc(sb_lp, 1)

                def attend(p):
                    pe.wait_ge(sb_att, 2 * (4 * l + p + 1))
                    if p == 0:
                        pe.wait_ge(out_read_act, out_reader(OUT_NO[l, "v", 1, 0])[1])
                        pe.wait_ge(dt_exp, l + 1)
                    if p >= 2:
                        pe.wait_ge(sb_lo, 4 * l + p - 1)
                    for a in range(2):
                        f = P * p + HD * a
                        o = ps[HD * a:HD * a + HD, 6 + p % 2, :]
                        pe.matmul(o[:, 0:S], va[:, 0, f:f + HD], sba[:, a, 0:S], start=True, stop=False,
                                  skip_group_check=True)
                        ins = pe.matmul(o[:, P:S], va[:, 1, f:f + HD], sba[:, a, S:S + P], start=False, stop=True,
                                        skip_group_check=True)
                    ins.then_inc(sb_y, 1)

                scores(0)
                scores(1)
                by_feature(l, "xbc", 4, u_hi, u_lo)
                log_between(0)
                by_feature(l, "xbc", 0, u_hi, u_lo)
                attend(0)
                scores(2)
                log_between(1)
                by_feature(l, "xbc", 1, u_hi, u_lo)
                attend(1)
                scores(3)
                log_between(2)
                by_feature(l, "xbc", 2, u_hi, u_lo)
                attend(2)
                log_between(3)
                by_feature(l, "xbc", 3, u_hi, u_lo)
                attend(3)

                by_feature(l, "ga", 0, u_hi, u_lo)
                pe.wait_ge(silued, 5 * l + 5)
                pe.wait_ge(sb_lo, 4 * l + 4)
                for g in range(2):
                    for c in range(2):
                        r, t = slice(64 * g, 64 * g + 64), slice(P * c, P * c + P)
                        pe.matmul(ps[:, 7 - g, P * (c + 1):P * (c + 1) + P], xc[r, 8, t], xc[r, 9, t],
                                  start=True, stop=True)
                pe.transpose(ps[:, 6, 0:P], xc[:, 8, 0:P], ident[:, :]).then_inc(b_turned, 1)
                for r in range(4):
                    t, g = r // 2, r % 2
                    for k in range(4):
                        ins = pe.transpose(ps[:, 2 + r, P * k:P * k + P], xc[:, 4 * g + k, P * t:P * t + P], ident[:, :])
                    ins.then_inc(x_turned, 1)
                by_feature(l, "ga", 1, u_hi, u_lo)

                def log_decays(c):
                    pe.wait_ge(a_tri, 2 * l + c + 1)
                    if c == 0:
                        pe.wait_ge(x_dt, 4 * l + 4)
                    else:
                        pe.wait_ge(yoff_read, 2 * l + 2)
                    for b in range(4):
                        ins = pe.matmul(ps[:, 2 + b, :], tri_gt[:, :], atri[:, 4 * b:4 * b + 4, :], start=True, stop=True)
                    ins.then_inc(seg, 1)

                def y_within(c):
                    pe.wait_ge(m_made, 4 * l + 2 * c + 2)
                    if c == 0:
                        pe.wait_ge(b_tok, l + 1)
                        pe.wait_ge(cb_made, 2 * l + 2)
                        pe.wait_ge(x_dt, 4 * l + 4)
                    else:
                        pe.wait_ge(y_read, 2 * l + 1)
                    for a in range(HEADS):
                        ins = pe.matmul(ps[:, 6 + a // 8, HD * (a % 8):HD * (a % 8) + HD], decay[:, a, :],
                                        xdt[:, c, HD * a:HD * a + HD], start=True, stop=True)
                    ins.then_inc(y_ps, 1)

                log_decays(0)
                by_feature(l, "ga", 2, u_hi, u_lo)
                pe.wait_ge(st_in, l + 1)
                pe.wait_ge(decayed, 2 * l + 1)
                pe.wait_ge(b_tok, l + 1)
                for g in range(2):
                    ins = pe.matmul(ps[64 * g:64 * g + 64, 2, :], btok[:, 64 * g:64 * g + 64],
                                    xdte[:, 512 * g:512 * g + 512], start=True, stop=True)
                ins.then_inc(st_ps, 1)
                by_feature(l, "ga", 3, u_hi, u_lo)
                y_within(0)
                pe.wait_ge(st_out, l + 1)
                for g in range(2):
                    r = slice(64 * g, 64 * g + 64)
                    ins = pe.matmul(ps[:, 2 + g, :], xc[r, 9, P:S], prev[r, :], start=True, stop=True)
                ins.then_inc(yoff_ps, 1)
                by_feature(l, "gb", 0, u_hi, u_lo)
                log_decays(1)
                by_feature(l, "gb", 1, u_hi, u_lo)
                y_within(1)
                by_feature(l, "gb", 2, u_hi, u_lo)
                by_feature(l, "gb", 3, u_hi, u_lo)
                for j in range(4):
                    by_token(l, "z", j, u_hi, u_lo)

                for j in range(2):
                    u = UNIT_OF[l, "sbo", j]
                    pe.wait_ge(sb_lo, 4 * l + 4)
                    for part in range(2):
                        o = begin(l, "sbo", j, part)
                        for f in range(2):
                            for k in range(4):
                                c = P * (2 * part + f)
                                ins = three(o[:, S * f:S * f + S], w(whi, u, k, c, P, 512), w(wlo, u, k, c, P, 512),
                                            o_hi[:, k, :], o_lo[:, k, :], k == 0, k == 3)
                        if part:
                            ins.then_inc(unit_used, 1)
                        else:
                            ins.then_inc(half_unit, 1)
                    if j == 0:
                        turn(l, N_SSD, decayed, 2 * l + 2)
                turned_ready(l, N_SSD)
                for j in range(4):
                    by_feature(l, "ssdo", j, m_hi, m_lo)
                turn(l, N_MEM, turned_lo, 8 * (l * NNORM + N_MEM))
                pe.wait_ge(merged_hi, 4 * l + 4)
                pe.wait_ge(merged_lo, 4 * l + 4)
                for j in range(4):
                    by_token(l, "wout", j, u_hi, u_lo)
                turned_ready(l, N_MEM)
                for j in range(2):
                    by_feature(l, "xk", j, m_hi, m_lo)
                turn(l, N_XA, turned_lo, 8 * (l * NNORM + N_XA))
                for j in range(2):
                    by_token(l, "xv", j, m_hi, m_lo)
                turned_ready(l, N_XA)
                for j in range(2):
                    by_feature(l, "xq", j, u_hi, u_lo)
                pe.wait_ge(out_read_act, out_reader(OUT_NO[l, "xq", 1, 0])[1])
                for a in range(XH):
                    for t in range(NT):
                        ins = pe.matmul(ps[:, 2 + a, S * t:S * t + S], qx[:, a, P * t:P * t + P], kx[:, a, :],
                                        start=True, stop=True)
                    ins.then_inc(xs_ps, 1)
                for a in range(XH + 1):
                    if a < XH:
                        pe.wait_ge(xs_p, 8 * l + 2 * a + 2)
                        for m in range(2):
                            for t in range(NT):
                                ins = pe.transpose(ps[:, 2 + a, S * m + P * t:S * m + P * t + P],
                                                   prob[:, 2 * a + t, P * m:P * m + P], ident[:, :])
                        ins.then_inc(xp_turned, 1)
                    if a:
                        b = a - 1
                        pe.wait_ge(xp_out, 4 * l + b + 1)
                        if b >= 2:
                            pe.wait_ge(xo_lo, 4 * l + b - 1)
                        else:
                            pe.wait_ge(y_read, 2 * l + 2)
                        for m in range(2):
                            ins = pe.matmul(ps[:, 6 + b % 2, 0:S], vx[:, m, P * b:P * b + P], pT[:, 2 * (b % 2) + m, :],
                                            start=(m == 0), stop=(m == 1))
                        ins.then_inc(xo_ps, 1)
                pe.wait_ge(xo_lo, 4 * l + 4)
                for j in range(2):
                    u = UNIT_OF[l, "xo", j]
                    for part in range(2):
                        o = begin(l, "xo", j, part)
                        for k in range(4):
                            ins = three(o, o_hi[:, k, P * part:P * part + P], o_lo[:, k, P * part:P * part + P],
                                        w(whi, u, k, 0, 512, 512), w(wlo, u, k, 0, 512, 512), k == 0, k == 3)
                        if part:
                            ins.then_inc(unit_used, 1)
                        else:
                            ins.then_inc(half_unit, 1)
                turn(l, N_FFN, turned_lo, 8 * (l * NNORM + N_FFN))
                turned_ready(l, N_FFN)
                if l == 0:
                    pe.wait_ge(out_read_dve, sum(o[0] == 0 and o[1] in BY_DVE for o in OUTS))

                    def gate_up(unit, c, which, first_use, slot):
                        pe.wait_ge(lo_made, unit + 1)
                        for f in range(2):
                            if which == 0 and not first_use:
                                pe.wait_ge(f_act, first_f_act(c) + f)
                            for k in range(KD):
                                a = k * 256 + P * f
                                ins = three(ps[:, bank_of(c, f), S * which:S * which + S],
                                            whi[:, slot, a:a + P], wlo[:, slot, a:a + P],
                                            u_hi[:, k, :], u_lo[:, k, :], k == 0, k == KD - 1)
                            if which:
                                ins.then_inc(unit_used if f else gu_ps, 1)
                            elif f:
                                ins.then_inc(unit_used, 1)

                    chunk_no = [0]

                    def bank_of(c, f):
                        return (2 * chunk_no[0] + f) % 4

                    def first_f_act(c):
                        return 2 * c - 3

                    def down(unit, c, parity, slot, start, stop):
                        pe.wait_ge(lo_made, unit + 1)
                        pe.wait_ge(f_lo, 2 * c + 2)
                        for t in range(NT):
                            for a in range(2):
                                for k in range(2):
                                    b = D * k + 512 * a
                                    ins = three(ps[:, 4 + 2 * t + a, :], hT_hi[:, parity, k, P * t:P * t + P],
                                                hT_lo[:, parity, k, P * t:P * t + P], whi[:, slot, b:b + 512],
                                                wlo[:, slot, b:b + 512], start and k == 0, stop and k == 1)
                        return ins

                    gate_up(FFN0, 0, 0, True, FFN0 % HL)
                    gate_up(FFN0 + 1, 0, 1, True, (FFN0 + 1) % HL)
                    for c in range(2):
                        chunk_no[0] = c + 1
                        gate_up(FFN0 + 3 * c + 2, c + 1, 0, c == 0, (FFN0 + 2) % HL)
                        gate_up(FFN0 + 3 * c + 3, c + 1, 1, c == 0, (FFN0 + 3) % HL)
                        down(FFN0 + 3 * c + 4, c, c % 2, (FFN0 + 4) % HL, c == 0, False).then_inc(unit_used, 1)
                    with pe.Fori(1, CH // 2) as i:
                        for half_ in range(2):
                            c = i * 2 + half_
                            chunk_no[0] = half_ + 1
                            gate_up(i * 6 + (FFN0 + 3 * half_ + 2), i * 2 + (half_ + 1), 0, False, (FFN0 + 2) % HL)
                            gate_up(i * 6 + (FFN0 + 3 * half_ + 3), i * 2 + (half_ + 1), 1, False, (FFN0 + 3) % HL)
                            down(i * 6 + (FFN0 + 3 * half_ + 4), c, half_, (FFN0 + 4) % HL, False, False)\
                                .then_inc(unit_used, 1)
                    ins = down(FFN0 + EU - 1, CH - 1, 0, (FFN0 + EU - 1) % HL, False, True)
                    ins.then_inc(unit_used, 1)

            pe.wait_ge(small_lo, 1)
            pe.wait_ge(xo_lo, 8)
            for t in range(NT):
                for k in range(KD):
                    c = slice(NE * k, NE * k + NE)
                    ins = three(ps[:, 6, NE * t:NE * t + NE], u_hi[:, k, P * t:P * t + P], u_lo[:, k, P * t:P * t + P],
                                wr_hi[:, c], wr_lo[:, c], k == 0, k == KD - 1)
            ins.then_inc(r_ps, 1)
            pe.wait_ge(r_mask, 1)
            mask = rt[:, 6]
            pe.matmul(ps[:, 7, 0:NE], tri_lt[:, :], mask[:, 0, :], start=True, stop=True)
            pe.matmul(ps[:, 7, NE:2 * NE], tri_lt[:, :], mask[:, 1, :], start=True, stop=False)
            pe.matmul(ps[:, 7, NE:2 * NE], one[:, :], mask[:, 0, :], start=False, stop=True)
            pe.matmul(ps[:, 7, 2 * NE:3 * NE], one[:, :], mask[:, 0, :], start=True, stop=False)
            pe.matmul(ps[:, 7, 2 * NE:3 * NE], one[:, :], mask[:, 1, :], start=False, stop=True).then_inc(r_rank, 1)
            pe.wait_ge(r_done, 1)
            n_visits = pe.value_load(visits_i[0:1, 0:1], min_val=NE, max_val=2 * NE)

            def gather(selected):
                pe.wait_ge(sel_made, selected)
                for r in range(2):
                    for k in range(4):
                        f = P * (4 * r + k)
                        o = ps[:, 6 + r, P * k:P * k + P]
                        for t in range(NT):
                            pe.matmul(o, mt_hi[:, t, f:f + P], sel[:, t, :], start=(t == 0), stop=False)
                            ins = pe.matmul(o, mt_lo[:, t, f:f + P], sel[:, t, :], start=False, stop=(t == 1))
                    ins.then_inc(ue_ps, 1)

            def scatter(i):
                t, a = i // 2, i % 2
                o = ps[:, 6 + a, :]
                pe.matmul(o, selT[:, P * t:P * t + P], y_hi[:, 512 * a:512 * a + 512], start=True, stop=False)
                pe.matmul(o, selT[:, P * t:P * t + P], y_lo[:, 512 * a:512 * a + 512], start=False, stop=True)\
                    .then_inc(e_sc, 1)

            pe.wait_ge(e_add, 1)
            gather(2)
            with pe.Fori(0, n_visits) as n:
                def gate_up_e(chunk, unit, j, par, which, wait_bank):
                    pe.wait_ge(lo_made, n * EU + (unit + 1))
                    if wait_bank:
                        pe.wait_ge(e_act, n * CH + (chunk - 1))
                    for k in range(KD):
                        ins = three(ps[:, par, 256 * which:256 * which + 256], ue_hi[:, k, :], ue_lo[:, k, :],
                                    w(whi, MOE0 + j, k, 0, 256, 256), w(wlo, MOE0 + j, k, 0, 256, 256),
                                    k == 0, k == KD - 1)
                    ins.then_inc(unit_used, 1)

                def turn_e(chunk, par):
                    pe.wait_ge(e_act, n * CH + (chunk + 1))
                    for f in range(2):
                        ins = pe.transpose(ps[:, 2 + par, P * f:P * f + P], act_f[:, par, P * f:P * f + P], ident[:, :])
                    ins.then_inc(e_turn, 1)

                def down_e(chunk, unit, j, par, start, stop):
                    pe.wait_ge(lo_made, n * EU + (unit + 1))
                    pe.wait_ge(e_lo, n * CH + (chunk + 1))
                    for a in range(2):
                        for k in range(2):
                            ins = three(ps[:, 4 + a, :], hT_hi[:, par, 0, P * k:P * k + P], hT_lo[:, par, 0, P * k:P * k + P],
                                        w(whi, MOE0 + j, k, 512 * a, 512, D), w(wlo, MOE0 + j, k, 512 * a, 512, D),
                                        start and k == 0, stop and k == 1)
                    ins.then_inc(unit_used, 1)
                    return ins

                def steps(i, c, before_up=None, before_down=None, start=False):
                    gate_up_e(i * 2 + (c + 1), i * 6 + (MOE0 + 3 * c + 2), 2, (c + 1) % 2, 0, not start or c)
                    turn_e(i * 2 + c, c)
                    if before_up:
                        before_up()
                    gate_up_e(i * 2 + (c + 1), i * 6 + (MOE0 + 3 * c + 3), 0, (c + 1) % 2, 1, False)
                    if before_down:
                        before_down()
                    down_e(i * 2 + c, i * 6 + (MOE0 + 3 * c + 4), 1, c, start and c == 0, False)

                def scatter_rest():
                    for i in range(2, 4):
                        pe.wait_ge(e_add, n * 4 + i)
                        scatter(i)

                def slots_of_this():
                    pe.wait_ge(e_add, n * 4 + 5)
                    for t in range(NT):
                        ins = pe.transpose(ps[:, 6, P * t:P * t + P], sel[:, t, :].bitcast(F32), ident[:, :])
                    ins.then_inc(selT_ps, 1)
                    for t in range(NT):
                        ins = pe.matmul(ps[:, 7, 0:1], sel[:, t, :].bitcast(F32), comb2[:, t, bass.ds(n, 1)],
                                        start=(t == 0), stop=(t == 1))
                    ins.then_inc(w_ps, 1)

                def gather_next():
                    pe.wait_ge(w_out_s, n + 1)
                    gather(2 * n + 4)
                    turn_e(CH - 1, 0)

                pe.wait_ge(ue_hi_out, 2 * n + 2)
                pe.wait_ge(ue_lo_out, 2 * n + 2)
                gate_up_e(0, MOE0, 0, 0, 0, False)
                gate_up_e(0, MOE0 + 1, 1, 0, 1, False)
                pe.wait_ge(e_yhi, n + 1)
                pe.wait_ge(e_ylo, n + 1)
                scatter(0)
                scatter(1)
                steps(0, 0, before_up=scatter_rest, before_down=slots_of_this, start=True)
                steps(0, 1, start=True)
                with pe.Fori(1, CH // 2 - 1) as i:
                    steps(i, 0)
                    steps(i, 1)
                steps(CH // 2 - 1, 0)
                steps(CH // 2 - 1, 1, before_down=gather_next)
                down_e(CH - 1, MOE0 + EU - 1, 2, 0, False, True)
            pe.wait_ge(e_yhi, n_visits + 1)
            pe.wait_ge(e_ylo, n_visits + 1)
            for i in range(4):
                if i == 0:
                    pe.wait_ge(ue_lo_out, n_visits * 2 + 2)
                if i >= 2:
                    pe.wait_ge(e_add, n_visits * 4 + i)
                scatter(i)


def unit_arrays(i):
    w_in = i["w_in"]
    col = {"z": 0, "xbc": D, "q": 2 * D + 272, "k": 2 * D + 784, "v": 2 * D + 1296,
           "ga": 2 * D + 1808, "gb": 3 * D + 1808}
    own = {"ssdo": "w_ssd_o", "wout": "w_out", "xk": "xa_wk", "xv": "xa_wv", "xq": "xa_wq",
           "sbo": "w_sb_o", "xo": "xa_wo"}

    def blocks(m, rows, cols, width):
        m = m[rows[0]:rows[1], cols:cols + width]
        return m.reshape(-1, P, width).transpose(1, 0, 2).reshape(P, UNIT)

    def mix_unit(l, name, j):
        if name in col:
            return blocks(w_in[l], (0, D), col[name] + 256 * j, 256)
        m = i[own[name]][l]
        width = UNIT * P // m.shape[0]
        return blocks(m, (0, m.shape[0]), width * j, width)

    def ffn_units(g, u, d):
        gate = [blocks(g, (0, D), 256 * c, 256) for c in range(CH)]
        up = [blocks(u, (0, D), 256 * c, 256) for c in range(CH)]
        dn = [blocks(d, (256 * c, 256 * c + 256), 0, D) for c in range(CH)]
        out = [gate[0], up[0]]
        for c in range(CH - 1):
            out += [gate[c + 1], up[c + 1], dn[c]]
        return out + [dn[CH - 1]]

    out = [mix_unit(0, *m) for m in MIX] + ffn_units(i["ffn_w_gate"][0], i["ffn_w_up"][0], i["ffn_w_down"][0])
    out += [mix_unit(1, *m) for m in MIX]
    for e in range(NE):
        out += ffn_units(i["moe_w_gate"][0, e], i["moe_w_up"][0, e], i["moe_w_down"][0, e])
    assert len(out) == NUNITS
    return np.stack(out)


def kernel(**inputs):
    import concourse.bacc as bacc
    from concourse.bass_utils import run_bass_kernel_spmd

    i = {k: np.asarray(v) for k, v in inputs.items()}

    def columns(v):
        return v.reshape(-1, P).T

    norms = ("norm_mix", "ssd_norm", "norm_mem", "norm_xa", "norm_ffn")
    arrays = {
        "x": i["x"][0], "mem": i["mem"][0], "units": unit_arrays(i),
        "w_dt": np.stack([i["w_in"][l][:, 2 * D + 256:2 * D + 272].reshape(KD, P, 16).transpose(1, 0, 2).reshape(P, -1)
                          for l in range(DEPTH)]),
        "w_router": i["moe_router"][0].reshape(KD, P, NE).transpose(1, 0, 2).reshape(P, -1),
        "gains": np.concatenate([columns(i[n][l]) for l in range(DEPTH) for n in norms], 1),
        "convw": np.concatenate([np.stack([columns(v) for v in (*i["conv_w"][l], i["conv_b"][l])], 2).reshape(P, -1)
                                 for l in range(DEPTH)], 1),
        "rows": np.concatenate([np.concatenate([i["dt_bias"][l], i["a_log"][l], i["d_skip"][l]]) for l in range(DEPTH)]),
        "ffn_row": i["norm_ffn"][1], "final_row": i["final_norm"],
    }
    arrays = {k: np.ascontiguousarray(v) for k, v in arrays.items()}
    nc = bacc.Bacc("TRN2", target_bir_lowering=False, num_devices=1)
    aps = [nc.dram_tensor(k, v.shape, mybir.dt.from_np(v.dtype), kind="ExternalInput").ap() for k, v in arrays.items()]
    out = nc.dram_tensor("out", (S, D), F32, kind="ExternalOutput").ap()
    trunk(nc, *aps, out)
    r = run_bass_kernel_spmd(nc, [arrays], core_ids=[0])
    return r.results[0]["out"].reshape(1, S, D)
```

```python
from contextlib import ExitStack

import numpy as np
import concourse.bass as bass
from concourse import mybir
from concourse.alu_op_type import AluOpType as ALU

F32 = mybir.dt.float32
F32R = mybir.dt.float32r
I32 = mybir.dt.int32
ACT = mybir.ActivationFunctionType
AX = mybir.AxisListType

P = 128
D = 1024
S = 256
NT = S // P
KD = D // P
DEPTH = 2
EPS = 1e-6
HEADS = 16
HD = 64
SBH = 8
XH = 4
CONV = 4
CT = 10
FF = 2816
NE = 8
CH = FF // 256
UNIT = 2048
RAW = 4
RAW_E = 7
HL = 3
NSEM = 11
EU = 3 * CH
PASS = NE * EU
AHEAD = 3
XSCALE = 128.0 ** -0.5
SPACE = 207 * 1024

MIX = ([("q", j) for j in range(2)] + [("k", j) for j in range(2)] + [("v", j) for j in range(2)]
       + [("xbc", j) for j in (4, 0, 1, 2, 3)] + [("ga", j) for j in range(4)] + [("gb", j) for j in range(4)]
       + [("z", j) for j in range(4)] + [("sbo", j) for j in range(2)] + [("ssdo", j) for j in range(4)]
       + [("wout", j) for j in range(4)] + [("xk", j) for j in range(2)] + [("xv", j) for j in range(2)]
       + [("xq", j) for j in range(2)] + [("xo", j) for j in range(2)])
NMIX = len(MIX)
FFN0 = NMIX
LAYER1 = FFN0 + EU
MOE0 = LAYER1 + NMIX
NUNITS = MOE0 + NE * EU
UNIT_OF = {(l, *m): (0, LAYER1)[l] + i for l in range(DEPTH) for i, m in enumerate(MIX)}

BY_DVE = ("sbo", "ssdo", "wout", "xo")
OUTS = [(l, n, j, part) for l in range(DEPTH) for n, j in MIX for part in range(2 if n in ("sbo", "xo") else 1)]
OUT_NO = {o: i for i, o in enumerate(OUTS)}


def slot_of(u):
    return (u - MOE0) % RAW if u < MOE0 else (u - MOE0 + RAW) % RAW_E


def out_reader(i):
    dve = OUTS[i][1] in BY_DVE
    return dve, sum((o[1] in BY_DVE) == dve for o in OUTS[:i + 1])


N_MIX, N_SSD, N_MEM, N_XA, N_FFN = range(5)
NNORM = 5


def trunk(nc, x, mem, units, w_dt, w_router, gains, convw, rows, ffn_row, final_row, out):
    ctx = ExitStack()
    with ctx:
        space = ctx.enter_context(nc.sbuf_tensor("space", [P, SPACE // 4], F32))
        base = nc.sbuf_base - SPACE
        at, top = {}, [0]

        def sb(name, shape, dt=F32, over=None, skip=0):
            size = 4 * int(np.prod(shape[1:]))
            size = (size + 31) // 32 * 32
            if over is None:
                at[name] = top[0]
                top[0] += size
                assert top[0] <= SPACE, (name, top[0])
            else:
                at[name] = at[over] + skip
            return nc.alloc_sbuf_tensor_at(name, shape, dt, offset=base + at[name])

        def sem(name):
            return ctx.enter_context(nc.semaphore(name))

        raw = sb("raw", [P, RAW, UNIT])
        raw_e = sb("raw_e", [P, RAW_E, UNIT], over="raw")
        xpad = sb("xpad", [P, CT * (S + CONV - 1)])
        zs = sb("zs", [P, 2, NT, 256])
        cbm = sb("cbm", [P, 2, 2, P])
        xtok = sb("xtok", [P, NT, D])
        assert at["xtok"] >= at["raw"] + 4 * UNIT * (RAW_E - 1) and RAW_E * UNIT * 4 <= at["xtok"] + 4 * NT * D
        whi = sb("whi", [P, HL, UNIT], F32R)
        wlo = sb("wlo", [P, HL, UNIT], F32R)
        u_hi = sb("u_hi", [P, KD, S], F32R)
        u_lo = sb("u_lo", [P, KD, S], F32R)
        m_hi = sb("m_hi", [P, KD, S], F32R)
        m_lo = sb("m_lo", [P, KD, S], F32R)
        o_hi = sb("o_hi", [P, 4, S], F32R)
        o_lo = sb("o_lo", [P, 4, S], F32R)
        h = sb("h", [P, NT, D])
        xn = sb("xn", [P, NT, D])
        xc = sb("xc", [P, CT, S])
        qk = sb("qk", [P, 8, S])
        sbw = sb("sbw", [P, 3, 2, 384])
        sbl, sbp, sba = sbw[:, 0], sbw[:, 1], sbw[:, 2]
        gb = sb("gb", [P, KD, S])
        hT_hi = sb("hT_hi", [P, 2, 2, S], F32R, over="qk")
        hT_lo = sb("hT_lo", [P, 2, 2, S], F32R, over="qk", skip=4096)
        sel = sb("sel", [P, NT, P], F32R, over="gb")
        selT = sb("selT", [P, S], F32R, over="gb", skip=2048)
        wdt = sb("wdt", [P, KD * 16])
        wdt_hi = sb("wdt_hi", [P, KD * 16], F32R)
        wdt_lo = sb("wdt_lo", [P, KD * 16], F32R)
        wr = sb("wr", [P, KD * NE])
        wr_hi = sb("wr_hi", [P, KD * NE], F32R)
        wr_lo = sb("wr_lo", [P, KD * NE], F32R)
        gain = sb("gain", [P, DEPTH * NNORM * KD])
        cw = sb("cw", [P, DEPTH * CT * (CONV + 1)])
        row = sb("row", [P, DEPTH * 3 * HEADS])
        ident = sb("ident", [P, P])
        tri_le = sb("tri_le", [P, P])
        tri_gt = sb("tri_gt", [P, P])
        tri_gt_r = sb("tri_gt_r", [P, P], F32R)
        a_hi = sb("a_hi", [P, NT, HEADS], F32R)
        a_lo = sb("a_lo", [P, NT, HEADS], F32R)
        neg_ge = sb("neg_ge", [P, P])
        tri_lt = sb("tri_lt", [P, P])
        neg_one = sb("neg_one", [P, P])
        one = sb("one", [P, P])
        iota = sb("iota", [P, P])
        first = sb("first", [P, NE])
        ss = sb("ss", [P, 64])
        ssy = sb("ssy", [P, NT, 2, 2])
        rs = sb("rs", [P, 64])
        half = sb("half", [P, 4])
        sdt = sb("sdt", [P, 7, NT, HEADS])
        eacum = sb("eacum", [P, 2, HEADS])
        btok = sb("btok", [P, P])
        xmx = sb("xmx", [P, 4, XH, NT])
        rt = sb("rt", [P, 12, NT, NE])
        rt1 = sb("rt1", [P, 8, NT])
        rank2 = sb("rank2", [P, NT, 2 * NE + 1])
        mask2 = sb("mask2", [P, NT, 2 * NE + 1])
        comb2 = sb("comb2", [P, NT, 2 * NE + 1])
        wslot = sb("wslot", [P, 1])
        silu_one = sb("silu_one", [P, 1])
        visits = sb("visits", [P, 4])
        visits_i = sb("visits_i", [P, 1], I32)

        ps = ctx.enter_context(nc.psum_tensor("ps", [P, 8, 512], F32))

        def flat(t):
            return t[:, :, :].rearrange("p a b -> p (a b)")

        xdt = xpad[:, 0:NT * D].rearrange("p (t f) -> p t f", t=NT)
        prev = xpad[:, NT * D:NT * D + 512]
        merged = xpad[:, 0:KD * S].rearrange("p (k s) -> p k s", k=KD)
        xconv = xpad[:, :].rearrange("p (c s) -> p c s", c=CT)
        decay = xc[:, 0:8, :].rearrange("p a (b t) -> p (a b) t", t=P)
        atri_hi = m_hi[:, :, :].rearrange("p a (b t) -> p (a b) t", t=P)
        atri_lo = m_lo[:, :, :].rearrange("p a (b t) -> p (a b) t", t=P)
        va = zs[:, :, :, :].rearrange("p a b c -> p (a b c)").rearrange("p (t f) -> p t f", t=NT)
        ga = sbw[:, :, :, :].rearrange("p a b c -> p (a b c)")[:, 0:KD * S].rearrange("p (k s) -> p k s", k=KD)
        xdte = flat(gb)[:, 0:D]
        yoff = flat(gb)[:, D:2 * D]
        kx, qx = xc[:, 0:4, :], xc[:, 4:8, :]
        vx = flat(qk)[:, 0:1024].rearrange("p (t f) -> p t f", t=NT)
        pT = qk[:, 4:8, :]
        prob = gb
        grow = flat(xc)[:, 0:D]
        frow = flat(xc)[:, D:2 * D]
        mt_hi = flat(m_hi).rearrange("p (t f) -> p t f", t=NT)
        mt_lo = flat(m_lo).rearrange("p (t f) -> p t f", t=NT)
        ue_hi = o_hi[:, :, :].rearrange("p a (b c) -> p (a b) c", c=P)
        ue_lo = o_lo[:, :, :].rearrange("p a (b c) -> p (a b) c", c=P)
        y_hi, y_lo = flat(u_hi)[:, 0:D], flat(u_lo)[:, 0:D]
        sg = sbl[:, :, 0:256]
        act_f = sbp[:, :, 0:256]
        by_head = sbw[0:HEADS, 0, 0, 0:S]
        by_expert = sbw[0:NE, 0, 0, 0:S]
        junk = qk

        landed = [sem(f"landed{i}") for i in range(NSEM)]
        hi_made, lo_made, unit_used = sem("hi_made"), sem("lo_made"), sem("unit_used")
        half_unit, unit_begun = sem("half_unit"), sem("unit_begun")
        out_read_act, out_read_dve = sem("out_read_act"), sem("out_read_dve")
        params_in, gain_in, mem_in = sem("params_in"), sem("gain_in"), sem("mem_in")
        h_in = [sem(f"h_in{t}") for t in range(NT)]
        ffn_half, wr_hi_made, wr_lo_made = sem("ffn_half"), sem("wr_hi_made"), sem("wr_lo_made")
        a_hi_made, a_lo_made, r_count, ut_lo = (sem(n) for n in ("a_hi_made", "a_lo_made", "r_count", "ut_lo"))
        dtT_ps, dtT_out, logitT_ps, logitT_out = (sem(n) for n in ("dtT_ps", "dtT_out", "logitT_ps", "logitT_out"))
        grow_in, frow_in = sem("grow_in"), sem("frow_in")
        consts, tri_r = sem("consts"), sem("tri_r")
        small_hi, small_lo = sem("small_hi"), sem("small_lo")
        small_raw, small_raw1 = sem("small_raw"), sem("small_raw1")
        sumsq, rstd, normed = sem("sumsq"), sem("rstd"), sem("normed")
        turned, turned_hi, turned_lo = sem("turned"), sem("turned_hi"), sem("turned_lo")
        q_out, v_out, x_out = sem("q_out"), sem("v_out"), sem("x_out")
        sb_z, sb_ln, sb_sp, sb_lp, sb_exp, sb_att, sb_y = (sem(n) for n in
            ("sb_z", "sb_ln", "sb_sp", "sb_lp", "sb_exp", "sb_att", "sb_y"))
        sb_hi, sb_lo = sem("sb_hi"), sem("sb_lo")
        dt_ps, dt_sum, dt_ln, dt_a, dt_cum, dt_exp = (sem(n) for n in
            ("dt_ps", "dt_sum", "dt_ln", "dt_a", "dt_cum", "dt_exp"))
        padded, conved, silued = sem("padded"), sem("conved"), sem("silued")
        x_turned, x_tok, x_dt, b_turned, b_tok = (sem(n) for n in ("x_turned", "x_tok", "x_dt", "b_turned", "b_tok"))
        a_tri, seg, decayed, cb_made, m_made = (sem(n) for n in
            ("a_tri", "seg", "decayed", "cb_made", "m_made"))
        y_ps, y_skip, y_read, st_in, st_ps, st_out, yoff_ps, yoff_read, yoff_added = (sem(n) for n in
            ("y_ps", "y_skip", "y_read", "st_in", "st_ps", "st_out", "yoff_ps", "yoff_read", "yoff_added"))
        z_silu, z_mul = sem("z_silu"), sem("z_mul")
        gates = sem("gates")
        merged_sum, merged_hi, merged_lo = sem("merged_sum"), sem("merged_hi"), sem("merged_lo")
        h_ffn = sem("h_ffn")
        kvx_out, xs_ps, xs_max, xs_exp, xs_p, xp_turned, xp_out, xo_ps, xo_hi, xo_lo = (sem(n) for n in
            ("kvx_out", "xs_ps", "xs_max", "xs_exp", "xs_p", "xp_turned", "xp_out", "xo_ps", "xo_hi", "xo_lo"))
        gu_ps, f_silu, f_act, f_hi, f_lo = (sem(n) for n in
            ("gu_ps", "f_silu", "f_act", "f_hi", "f_lo"))
        r_ps, r_mask, r_exp, r_rank, r_done, r_twice, ut_made, ut_hi = (sem(n) for n in
            ("r_ps", "r_mask", "r_exp", "r_rank", "r_done", "r_twice", "ut_made", "ut_hi"))
        sel_made, selT_ps, selT_out, ue_ps, ue_hi_out, ue_lo_out = (sem(n) for n in
            ("sel_made", "selT_ps", "selT_out", "ue_ps", "ue_hi_out", "ue_lo_out"))
        w_ps, w_out_s = sem("w_ps"), sem("w_out_s")
        e_silu, e_act, e_turn, e_hi, e_lo, e_yhi, e_ylo, e_sc, e_add = (sem(n) for n in
            ("e_silu", "e_act", "e_turn", "e_hi", "e_lo", "e_yhi", "e_ylo", "e_sc", "e_add"))
        final_made, stored = sem("final_made"), sem("stored")
        act_chain, dve_chain, pool_chain = sem("act_chain"), sem("dve_chain"), sem("pool_chain")

        def chain(eng, s):
            count = [0]

            def link(ins):
                count[0] += 1
                ins.then_inc(s, 1)
                eng.wait_ge(s, count[0])
            return link

        def gcol(l, n, k):
            i = (l * NNORM + n) * KD + k
            return gain[:, i:i + 1]

        def rowof(l, i):
            a = (l * 3 + i) * HEADS
            return row[:, a:a + HEADS]

        def sums_before(n):
            return 2 * n + 6 * ((n + NNORM - 1 - N_SSD) // NNORM)

        def down_unit(c):
            return 3 * c + 4 if c < CH - 1 else EU - 1

        def up_unit(c):
            return 3 * c if c else 1

        def raw_at(u):
            return (raw if u < MOE0 else raw_e)[:, slot_of(u), :]

        block = ctx.enter_context(nc.Block())

        @block.sync
        def _(sp):
            def load(u):
                sp.dma_start(raw_at(u), units[u]).then_inc(landed[u % NSEM], 16)

            def load_experts(first, groups, again=0):
                with sp.Fori(0, groups) as g:
                    for j in range(NSEM):
                        slot = sp.snap((g * NSEM + (first + j - MOE0 + RAW)) % RAW_E)
                        unit = sp.snap(g * NSEM + (first + j - again))
                        free = sp.snap(g * NSEM + (first + j - RAW_E + 1))
                        sp.wait_ge(lo_made, free)
                        sp.dma_start(raw_e[:, bass.ds(slot, 1), :], units[bass.ds(unit, 1)].rearrange("u p n -> p u n"))\
                            .then_inc(landed[(first + j) % NSEM], 16)

            def load_again(first, count, again):
                for u in range(first, first + count):
                    sp.wait_ge(lo_made, u - RAW_E + 1)
                    sp.dma_start(raw_at(u), units[u - again]).then_inc(landed[u % NSEM], 16)

            sp.dma_start(h[:, 0, :], x[0:P, :]).then_inc(h_in[0], 16)
            sp.dma_start(gain[:, :], gains[:, :]).then_inc(gain_in, 16)
            sp.dma_start(h[:, 1, :], x[P:S, :]).then_inc(h_in[1], 16)
            sp.dma_start(wdt[:, :], w_dt[0]).then_inc(small_raw, 16)
            load(0)
            load(1)
            sp.dma_start(row[:, :], rows.partition_broadcast(P)).then_inc(params_in, 16)
            sp.dma_start(cw[:, :], convw[:, :]).then_inc(params_in, 16)
            sp.dma_start(wr[:, :], w_router[:, :]).then_inc(params_in, 16)
            for u in range(2, NSEM):
                if u >= RAW:
                    sp.wait_ge(lo_made, u - RAW + 1)
                load(u)
            with sp.Fori(1, MOE0 // NSEM) as g:
                for j in range(NSEM):
                    slot = sp.snap((g * NSEM + (j + RAW - MOE0 % RAW)) % RAW)
                    unit = sp.snap(g * NSEM + j)
                    free = sp.snap(g * NSEM + (j - RAW + 1))
                    sp.wait_ge(lo_made, free)
                    sp.dma_start(raw[:, bass.ds(slot, 1), :], units[bass.ds(unit, 1)].rearrange("u p n -> p u n"))\
                        .then_inc(landed[j], 16)
            for u in range(MOE0 // NSEM * NSEM, MOE0):
                sp.wait_ge(lo_made, u - RAW + 1)
                load(u)
            for u in range(MOE0, MOE0 + NSEM):
                sp.wait_ge(lo_made, u - RAW_E + 1)
                if slot_of(u) == RAW_E - 1 and u < MOE0 + RAW_E:
                    sp.wait_ge(ut_lo, NT)
                load(u)
            load_experts(MOE0 + NSEM, NE * EU // NSEM - 1)
            load_again(NUNITS, AHEAD, PASS)
            sp.wait_ge(r_done, 1)
            n_visits = sp.value_load(visits_i[0:1, 0:1], min_val=NE, max_val=2 * NE)
            with sp.If(n_visits > NE):
                load_experts(NUNITS + AHEAD, PASS // NSEM - 1, PASS)
                rest = NUNITS + AHEAD + PASS - NSEM
                load_again(rest, NSEM - AHEAD, PASS)
                load_again(NUNITS + PASS, AHEAD, 2 * PASS)
            for t in range(NT):
                sp.wait_ge(final_made, t + 1)
                sp.dma_start(out[P * t:P * t + P, :], xn[:, t, :]).then_inc(stored, 16)
            sp.wait_ge(stored, 16 * NT)

        @block.gpsimd
        def _(gp):
            link = chain(gp, pool_chain)
            gp.memset(half[:, :], -0.5).then_inc(consts, 1)
            for m, v in ((ident, 0.0), (tri_le, 1.0), (tri_gt, 1.0), (neg_ge, -1.0), (tri_lt, 1.0)):
                link(gp.memset(m[:, :], v))
            gp.memset(neg_one[:, :], -1.0).then_inc(consts, 1)
            gp.memset(one[:, :], 1.0).then_inc(consts, 1)
            for m, op, fill, step in ((ident, ALU.not_equal, 1.0, -1), (tri_le, ALU.is_ge, 0.0, 1),
                                      (tri_gt, ALU.is_gt, 0.0, -1), (neg_ge, ALU.is_ge, 0.0, -1),
                                      (tri_lt, ALU.is_gt, 0.0, 1)):
                gp.affine_select(out=m[:, :], in_=m[:, :], compare_op=op, fill=fill, base=0,
                                 pattern=[[step, P]], channel_multiplier=-step).then_inc(consts, 1)
            gp.iota(iota[:, :], pattern=[[1, P]], base=0, channel_multiplier=0,
                    allow_small_or_imprecise_dtypes=True).then_inc(consts, 1)
            gp.iota(first[:, :], pattern=[[-1, NE]], base=NE, channel_multiplier=0,
                    allow_small_or_imprecise_dtypes=True).then_inc(consts, 1)
            gp.wait_ge(consts, 10)

            def root(n):
                for t in range(NT):
                    if n % NNORM == N_SSD and n < DEPTH * NNORM:
                        cols, width = 2, D // 2
                        c = slice(4 * n + 2 * t, 4 * n + 2 * t + 2)
                        gp.wait_ge(sumsq, sums_before(n) + 7 + t)
                        link(gp.tensor_tensor(out=ss[:, c], in0=ssy[:, t, :, 0], in1=ssy[:, t, :, 1], op=ALU.add))
                    else:
                        cols, width = 1, D
                        c = slice(4 * n + t, 4 * n + t + 1)
                        gp.wait_ge(sumsq, sums_before(n) + 1 + t)
                    link(gp.tensor_scalar(ss[:, c], ss[:, c], 1.0 / width, EPS, ALU.mult, ALU.add))
                    gp.tensor_tensor(out=rs[:, c], in0=ss[:, c], in1=half[:, 0:cols], op=ALU.pow).then_inc(rstd, 1)

            for l in range(DEPTH):
                root(l * NNORM + N_MIX)
                if l:
                    gp.wait_ge(small_lo, 1)
                    gp.dma_start(wdt[:, :], w_dt[l]).then_inc(small_raw1, 16)
                gp.wait_ge(params_in, 48)
                if l:
                    gp.wait_ge(sb_z, 4 * l + 1)
                gp.wait_ge(a_lo_made, l + 1)
                for c in range(2):
                    if c == 1:
                        gp.wait_ge(seg, 2 * l + 1)
                    for part, dst in ((a_hi, atri_hi), (a_lo, atri_lo)):
                        gp.tensor_tensor(out=dst, in0=tri_le[:, :].unsqueeze(1).to_broadcast([P, HEADS, P]),
                                         in1=part[:, c, :].bitcast(F32).unsqueeze(2).to_broadcast([P, HEADS, P]),
                                         op=ALU.mult).then_inc(a_tri, 1)
                    if c == 0:
                        gp.wait_ge(x_tok, 4 * l + 4)
                        gp.wait_ge(turned, 4 * (l * NNORM + N_MIX + 1))
                        for t in range(NT):
                            gp.tensor_tensor(out=xn[:, t, :].rearrange("p (h d) -> p h d", h=HEADS),
                                             in0=xtok[:, t, :].rearrange("p (h d) -> p h d", h=HEADS),
                                             in1=rowof(l, 2).unsqueeze(2).to_broadcast([P, HEADS, HD]),
                                             op=ALU.mult).then_inc(y_skip, 1)
                gp.wait_ge(y_skip, 2 * l + 2)
                gp.dma_start(xtok[:, :, :], mem.rearrange("(t p) d -> p t d", p=P)).then_inc(mem_in, 16)
                root(l * NNORM + N_SSD)
                root(l * NNORM + N_MEM)
                root(l * NNORM + N_XA)
                if l == DEPTH - 1:
                    gp.wait_ge(xs_ps, 4 * DEPTH)
                    gp.dma_start(grow, ffn_row.partition_broadcast(P)).then_inc(grow_in, 16)
                    gp.dma_start(frow, final_row.partition_broadcast(P)).then_inc(frow_in, 16)
                root(l * NNORM + N_FFN)
            gp.wait_ge(grow_in, 16)
            for t in range(NT):
                gp.wait_ge(normed, 2 * (DEPTH - 1) * NNORM + 2 * N_FFN + t + 1)
                gp.tensor_tensor(out=xtok[:, t, :], in0=xn[:, t, :], in1=grow, op=ALU.mult).then_inc(ut_made, 1)
            for t in range(NT):
                gp.wait_ge(ut_hi, t + 1)
                gp.tensor_tensor(out=mt_lo[:, t, :], in0=xtok[:, t, :], in1=mt_hi[:, t, :].bitcast(F32),
                                 op=ALU.subtract).then_inc(ut_lo, 1)
            root(DEPTH * NNORM)

        @block.scalar
        def _(act):
            link = chain(act, act_chain)
            made = [0]

            def split(u):
                act.wait_ge(landed[u % NSEM], 16 * (u // NSEM + 1))
                if u >= HL:
                    act.wait_ge(unit_used, u - HL + 1)
                act.activation(whi[:, u % HL, :], raw_at(u), ACT.Copy).then_inc(hi_made, 1)

            def feed(upto):
                for u in range(made[0], min(upto, MOE0 + AHEAD - 1) + 1):
                    split(u)
                made[0] = max(made[0], min(upto, MOE0 + AHEAD - 1) + 1)

            def result(l, name, j, part=0):
                u = UNIT_OF[l, name, j]
                feed(u + 2)
                act.wait_ge(unit_used, u + 1)
                return ps[:, OUT_NO[l, name, j, part] % 2, :]

            def squares(l, n, src, ready=None):
                i = l * NNORM + n
                act.wait_ge(turned, 4 * i)
                for t in range(NT):
                    if ready:
                        act.wait_ge(*ready(t))
                    act.activation(xn[:, t, :], src[:, t, :], ACT.Square,
                                   accum_out=ss[:, 4 * i + t:4 * i + t + 1]).then_inc(sumsq, 1)

            def turn_hi(l, n, dst):
                i = l * NNORM + n
                for r in range(4):
                    act.wait_ge(turned, 4 * i + r + 1)
                    for k in range(2):
                        act.activation(dst[:, 2 * r + k, :], ps[:, 2 + r, k * S:(k + 1) * S], ACT.Copy,
                                       scale=gcol(l, n, 2 * r + k)).then_inc(turned_hi, 1)

            act.wait_ge(consts, 10)
            act.activation(tri_gt_r[:, :], tri_gt[:, :], ACT.Copy).then_inc(tri_r, 1)
            for l in range(DEPTH):
                squares(l, N_MIX, h, lambda t: (h_ffn, 2 * t + 2) if l else (h_in[t], 16))
                act.wait_ge(small_raw1 if l else small_raw, 16)
                act.activation(wdt_hi[:, :], wdt[:, :], ACT.Copy).then_inc(small_hi, 1)
                if l == 0:
                    feed(0)
                    act.wait_ge(gain_in, 16)
                turn_hi(l, N_MIX, u_hi)
                feed(UNIT_OF[l, "q", 0] + 2)
                if l == 0:
                    act.wait_ge(params_in, 48)
                    act.activation(wr_hi[:, :], wr[:, :], ACT.Copy).then_inc(wr_hi_made, 1)
                act.activation(sdt[:, 4, 0, :], rowof(l, 1), ACT.Exp).then_inc(small_hi, 1)
                for n, j in [("q", 0), ("q", 1), ("k", 0), ("k", 1)]:
                    o = result(l, n, j)
                    c = (0 if n == "q" else 4) + 2 * j
                    act.activation(qk[:, c:c + 2, :], o.rearrange("p (a b) -> p a b", a=2), ACT.Copy,
                                   scale=(HD ** -0.5 if n == "q" else 1.0)).then_inc(out_read_act, 1)
                    if (n, j) == ("q", 1):
                        feed(UNIT_OF[l, "k", 0] + 2)
                        act.wait_ge(dt_sum, l + 1)
                        link(act.activation(sdt[:, 1, :, :], sdt[:, 0, :, :], ACT.Abs))
                        link(act.activation(sdt[:, 1, :, :], sdt[:, 1, :, :], ACT.Exp, scale=-1.0))
                        act.activation(sdt[:, 1, :, :], sdt[:, 1, :, :], ACT.Ln, bias=1.0).then_inc(dt_ln, 1)
                        act.wait_ge(dt_a, l + 1)
                        if l:
                            act.wait_ge(a_tri, 4 * l)
                        act.activation(a_hi[:, :, :], sdt[:, 3, :, :], ACT.Copy).then_inc(a_hi_made, 1)
                for j in range(2):
                    o = result(l, "v", j)
                    act.activation(va[:, :, 256 * j:256 * j + 256], o.rearrange("p (a b) -> p a b", a=2),
                                   ACT.Copy).then_inc(out_read_act, 1)
                act.wait_ge(dt_cum, l + 1)
                act.activation(eacum[:, :, :], ps[:, 7, 64:96].rearrange("p (a b) -> p a b", a=2),
                               ACT.Exp).then_inc(dt_exp, 1)

                def softplus_tail(p):
                    z = ps[:, 2 + 2 * (p % 2):4 + 2 * (p % 2), 0:384]
                    act.wait_ge(sb_z, 4 * l + p + 1)
                    if 4 * l + p >= 1:
                        act.wait_ge(sb_sp, 4 * l + p)
                    link(act.activation(sbl[:, :, :], z, ACT.Abs))
                    link(act.activation(sbl[:, :, :], sbl[:, :, :], ACT.Exp, scale=-1.0))
                    act.activation(sbl[:, :, :], sbl[:, :, :], ACT.Ln, bias=1.0).then_inc(sb_ln, 1)

                def exp_att(p):
                    act.wait_ge(sb_lp, 4 * l + p + 1)
                    if 4 * l + p >= 1:
                        act.wait_ge(sb_y, 4 * l + p)
                    act.activation(sba[:, :, :], ps[:, 2 + 2 * (p % 2):4 + 2 * (p % 2), 0:384],
                                   ACT.Exp).then_inc(sb_exp, 1)

                def y_out(p):
                    act.wait_ge(sb_y, 4 * l + p + 1)
                    act.activation(o_hi[:, p, :], ps[:, 6 + p % 2, 0:S], ACT.Copy).then_inc(sb_hi, 1)

                def pad(n):
                    j = (4, 0, 1, 2, 3)[n]
                    o = result(l, "xbc", j)
                    if l and n == 0:
                        act.wait_ge(merged_hi, 4 * l)
                        act.wait_ge(merged_lo, 4 * l)
                    act.activation(xconv[:, 2 * j:2 * j + 2, CONV - 1:], o.rearrange("p (a b) -> p a b", a=2),
                                   ACT.Copy).then_inc(out_read_act, 1)

                def silu(n):
                    j = (4, 0, 1, 2, 3)[n]
                    act.wait_ge(conved, 5 * l + n + 1)
                    act.activation(xc[:, 2 * j:2 * j + 2, :], xc[:, 2 * j:2 * j + 2, :],
                                   ACT.Silu).then_inc(silued, 1)

                softplus_tail(0)
                softplus_tail(1)
                exp_att(0)
                pad(0)
                exp_att(1)
                pad(1)
                softplus_tail(2)
                y_out(0)
                pad(2)
                softplus_tail(3)
                exp_att(2)
                pad(3)
                y_out(1)
                exp_att(3)
                pad(4)
                silu(0)
                y_out(2)
                y_out(3)
                def gate(name, j):
                    o = result(l, name, j)
                    if name == "gb" and j < 2:
                        act.wait_ge(st_ps, l + 1)
                    if name == "gb" and j >= 2:
                        act.wait_ge(yoff_added, l + 1)
                    act.activation((ga if name == "ga" else gb)[:, 2 * j:2 * j + 2, :],
                                   o.rearrange("p (a b) -> p a b", a=2), ACT.Tanh,
                                   scale=0.5).then_inc(out_read_act, 1)

                def decays(c):
                    act.wait_ge(seg, 2 * l + c + 1)
                    if c == 1:
                        act.wait_ge(y_ps, 2 * l + 1)
                    act.activation(decay, ps[:, 2:6, :].rearrange("p a (b t) -> p (a b) t", t=P),
                                   ACT.Exp).then_inc(decayed, 1)

                act.wait_ge(sb_y, 4 * l + 4)
                gate("ga", 0)
                for n in range(1, 5):
                    silu(n)
                gate("ga", 1)
                act.wait_ge(b_turned, l + 1)
                act.activation(btok[:, :], ps[:, 6, 0:P], ACT.Copy).then_inc(b_tok, 1)
                if l:
                    act.wait_ge(normed, 2 * ((l - 1) * NNORM + N_MEM + 1))
                for r in range(4):
                    act.wait_ge(x_turned, 4 * l + r + 1)
                    act.activation(xtok[:, r // 2, (r % 2) * 512:(r % 2) * 512 + 512], ps[:, 2 + r, :],
                                   ACT.Copy).then_inc(x_tok, 1)
                gate("ga", 2)
                decays(0)
                gate("ga", 3)
                act.wait_ge(st_ps, l + 1)
                act.activation(prev, ps[:, 2, :], ACT.Copy).then_inc(st_out, 1)
                gate("gb", 0)
                gate("gb", 1)
                decays(1)
                gate("gb", 2)
                gate("gb", 3)
                for j in range(4):
                    o = result(l, "z", j)
                    if 4 * l + j >= 2:
                        act.wait_ge(z_mul, 4 * l + j - 1)
                    act.activation(zs[:, j % 2, :, :], o.rearrange("p (a b) -> p a b", a=2),
                                   ACT.Silu).then_inc(out_read_act, 1)
                    act.wait_ge(z_mul, 4 * l + j + 1)
                    for t in range(NT):
                        act.activation(junk[:, 2 * j + t, :], xn[:, t, 256 * j:256 * j + 256], ACT.Square,
                                       accum_out=ssy[:, t, j // 2, j % 2:j % 2 + 1]).then_inc(sumsq, 1)
                feed(UNIT_OF[l, "ssdo", 0])
                turn_hi(l, N_SSD, m_hi)
                feed(UNIT_OF[l, "ssdo", 1])
                act.wait_ge(mem_in, 16 * (l + 1))
                squares(l, N_MEM, xtok)
                for j in range(4):
                    feed(UNIT_OF[l, "ssdo", j] + (3 if j < 3 else 2))
                    act.wait_ge(merged_sum, 4 * l + j + 1)
                    act.activation(u_hi[:, 2 * j:2 * j + 2, :], merged[:, 2 * j:2 * j + 2, :], ACT.Copy,
                                   scale=0.5).then_inc(merged_hi, 1)
                turn_hi(l, N_MEM, m_hi)
                feed(UNIT_OF[l, "wout", 3] + 2)
                act.wait_ge(out_read_dve, out_reader(OUT_NO[l, "wout", 3, 0])[1])
                squares(l, N_XA, h)
                for j in range(2):
                    o = result(l, "xk", j)
                    act.activation(kx[:, 2 * j:2 * j + 2, :], o.rearrange("p (a b) -> p a b", a=2),
                                   ACT.Copy).then_inc(out_read_act, 1)
                turn_hi(l, N_XA, u_hi)
                for j in range(2):
                    o = result(l, "xv", j)
                    act.activation(vx[:, :, 256 * j:256 * j + 256], o.rearrange("p (a b) -> p a b", a=2),
                                   ACT.Copy).then_inc(out_read_act, 1)
                for j in range(2):
                    o = result(l, "xq", j)
                    act.activation(qx[:, 2 * j:2 * j + 2, :], o.rearrange("p (a b) -> p a b", a=2),
                                   ACT.Copy).then_inc(out_read_act, 1)
                for a in range(XH):
                    act.wait_ge(xs_max, 4 * l + a + 1)
                    for t in range(NT):
                        act.activation(prob[:, 2 * a + t, :], ps[:, 2 + a, t * S:(t + 1) * S], ACT.Exp,
                                       scale=XSCALE, bias=xmx[:, 1, a, t:t + 1],
                                       accum_out=xmx[:, 2, a, t:t + 1]).then_inc(xs_exp, 1)
                for a in range(XH):
                    act.wait_ge(xp_turned, 4 * l + a + 1)
                    if 4 * l + a >= 2:
                        act.wait_ge(xo_ps, 4 * l + a - 1)
                    act.activation(pT[:, 2 * (a % 2):2 * (a % 2) + 2, :],
                                   ps[:, 2 + a, :].rearrange("p (a b) -> p a b", a=2), ACT.Copy).then_inc(xp_out, 1)
                    if a >= 1:
                        act.wait_ge(xo_ps, 4 * l + a)
                        act.activation(o_hi[:, a - 1, :], ps[:, 6 + (a - 1) % 2, 0:S], ACT.Copy).then_inc(xo_hi, 1)
                act.wait_ge(xo_ps, 4 * l + 4)
                act.activation(o_hi[:, 3, :], ps[:, 7, 0:S], ACT.Copy).then_inc(xo_hi, 1)
                feed(UNIT_OF[l, "xo", 1] + 1)
                squares(l, N_FFN, h, lambda t: (out_read_dve, out_reader(OUT_NO[l, "xo", 1, t])[1]))
                turn_hi(l, N_FFN, u_hi)
                if l == 0:
                    for c in range(CH):
                        for f in range(2):
                            n = 2 * c + f
                            feed(FFN0 + up_unit(c) + 2)
                            if f == 0:
                                act.wait_ge(gu_ps, c + 1)
                            else:
                                act.wait_ge(unit_used, FFN0 + up_unit(c) + 1)
                            if n >= 2:
                                act.wait_ge(f_act, n - 1)
                            else:
                                act.wait_ge(out_read_dve, sum(o[0] == 0 and o[1] in BY_DVE for o in OUTS))
                            act.activation(sg[:, f, :], ps[:, n % 4, 0:S], ACT.Silu).then_inc(f_silu, 1)
                        if c >= 2:
                            act.wait_ge(unit_used, FFN0 + down_unit(c - 2) + 1)
                        for f in range(2):
                            act.wait_ge(f_act, 2 * c + f + 1)
                            act.activation(hT_hi[:, c % 2, f, :], act_f[:, f, :], ACT.Copy).then_inc(f_hi, 1)
                    feed(LAYER1 + 1)

            for t in range(NT):
                act.wait_ge(ut_made, t + 1)
                act.activation(mt_hi[:, t, :], xtok[:, t, :], ACT.Copy).then_inc(ut_hi, 1)
            feed(MOE0 + 1)
            act.wait_ge(r_mask, 1)
            act.activation(rt1[:, 4, :], rt1[:, 3, :], ACT.Exp).then_inc(r_exp, 1)

            def gathered(count, r):
                act.wait_ge(ue_ps, count)
                act.activation(ue_hi[:, 4 * r:4 * r + 4, :], ps[:, 6 + r, :].rearrange("p (a b) -> p a b", a=4),
                               ACT.Copy).then_inc(ue_hi_out, 1)

            def y_half(used):
                act.wait_ge(unit_used, used)
                act.activation(y_hi, ps[:, 4:6, :].rearrange("p a b -> p (a b)"), ACT.Copy,
                               scale=wslot[:, 0:1]).then_inc(e_yhi, 1)

            act.wait_ge(r_done, 1)
            n_visits = act.value_load(visits_i[0:1, 0:1], min_val=NE, max_val=2 * NE)
            for r in range(2):
                gathered(r + 1, r)
            y_half(MOE0)
            feed(MOE0 + AHEAD - 1)
            with act.Fori(0, n_visits) as n:
                slots = [act.snap((n * EU + (RAW + s)) % RAW_E) for s in range(RAW_E)]

                def split_e(j):
                    act.wait_ge(landed[(MOE0 + j) % NSEM], n * (16 * EU // NSEM) + 16 * ((MOE0 + j) // NSEM + 1))
                    act.wait_ge(unit_used, n * EU + (MOE0 + j - HL + 1))
                    act.sem_inc(unit_begun, 1)
                    act.activation(whi[:, (MOE0 + j) % HL, :], raw_e[:, bass.ds(slots[j % RAW_E], 1), :],
                                   ACT.Copy).then_inc(hi_made, 1)

                act.activation(silu_one[:, :], one[:, 0:1], ACT.Silu)
                for c in range(CH):
                    if c:
                        split_e(3 * c + 2)
                    if c == 1:
                        act.wait_ge(selT_ps, n + 1)
                        act.activation(selT[:, :], ps[:, 6, 0:S], ACT.Copy).then_inc(selT_out, 1)
                        act.wait_ge(w_ps, n + 1)
                        act.activation(wslot[:, :], ps[:, 7, 0:1], ACT.Copy).then_inc(w_out_s, 1)
                    act.wait_ge(unit_used, n * EU + (MOE0 + up_unit(c) + 1))
                    if c >= 2:
                        act.wait_ge(e_act, n * CH + (c - 1))
                    act.activation(sg[:, c % 2, :], ps[:, c % 2, 0:256], ACT.Silu).then_inc(e_silu, 1)
                    if 3 * c + 3 < EU:
                        split_e(3 * c + 3)
                    if c and 3 * c + 4 < EU:
                        split_e(3 * c + 4)
                    if c == CH - 1:
                        for r in range(2):
                            gathered(2 * n + (r + 3), r)
                    act.wait_ge(e_turn, n * CH + (c + 1))
                    act.activation(hT_hi[:, c % 2, 0, :], ps[:, 2 + c % 2, 0:256], ACT.Copy).then_inc(e_hi, 1)
                    if c == 0:
                        split_e(4)
                split_e(EU)
                split_e(EU + 1)
                y_half(n * EU + (MOE0 + EU))
                split_e(EU + 2)
            i = DEPTH * NNORM
            for t in range(NT):
                act.wait_ge(e_add, n_visits * 4 + (2 * t + 3))
                act.activation(xn[:, t, :], h[:, t, :], ACT.Square,
                               accum_out=ss[:, 4 * i + t:4 * i + t + 1]).then_inc(sumsq, 1)

        @block.vector
        def _(dve):
            link = chain(dve, dve_chain)
            made = [0]

            def split(u):
                dve.wait_ge(hi_made, u + 1)
                dve.tensor_tensor(out=wlo[:, u % HL, :], in0=raw_at(u),
                                  in1=whi[:, u % HL, :].bitcast(F32), op=ALU.subtract).then_inc(lo_made, 1)

            def feed(upto):
                for u in range(made[0], min(upto, MOE0 + AHEAD - 1) + 1):
                    split(u)
                made[0] = max(made[0], min(upto, MOE0 + AHEAD - 1) + 1)

            def result(l, name, j, part=0):
                u = UNIT_OF[l, name, j]
                feed(u + 2)
                dve.wait_ge(unit_used, u + 1)
                return ps[:, OUT_NO[l, name, j, part] % 2, :]

            def normalise(l, n, src):
                i = l * NNORM + n
                for t in range(NT):
                    dve.wait_ge(rstd, 2 * i + t + 1)
                    dve.tensor_scalar(xn[:, t, :], src[:, t, :], rs[:, 4 * i + t:4 * i + t + 1], None,
                                      ALU.mult).then_inc(normed, 1)

            def turn_lo(l, n, hi, lo):
                i = l * NNORM + n
                for r in range(4):
                    dve.wait_ge(turned_hi, 8 * i + 2 * r + 2)
                    for k in range(2):
                        dve.scalar_tensor_tensor(lo[:, 2 * r + k, :], ps[:, 2 + r, k * S:(k + 1) * S],
                                                 gcol(l, n, 2 * r + k), hi[:, 2 * r + k, :].bitcast(F32),
                                                 ALU.mult, ALU.subtract).then_inc(turned_lo, 1)

            for l in range(DEPTH):
                if l == 0:
                    for t in range(NT):
                        dve.wait_ge(h_in[t], 16)
                normalise(l, N_MIX, h)
                dve.wait_ge(small_hi, 2 * l + 1)
                dve.tensor_tensor(out=wdt_lo[:, :], in0=wdt[:, :], in1=wdt_hi[:, :].bitcast(F32),
                                  op=ALU.subtract).then_inc(small_lo, 1)
                if l == 0:
                    feed(0)
                turn_lo(l, N_MIX, u_hi, u_lo)
                feed(UNIT_OF[l, "q", 0] + 2)
                dve.wait_ge(dtT_ps, l + 1)
                dve.tensor_copy(by_head, ps[0:HEADS, 7, 0:S]).then_inc(dtT_out, 1)
                if l == 0:
                    dve.wait_ge(wr_hi_made, 1)
                    dve.tensor_tensor(out=wr_lo[:, :], in0=wr[:, :], in1=wr_hi[:, :].bitcast(F32),
                                      op=ALU.subtract).then_inc(wr_lo_made, 1)
                    dve.wait_ge(params_in, 48)
                feed(UNIT_OF[l, "q", 1] + 2)
                dve.wait_ge(small_hi, 2 * l + 2)
                dve.wait_ge(dt_ps, l + 1)
                link(dve.tensor_tensor(out=sdt[:, 0, :, :], in0=ps[:, 7, 0:32].rearrange("p (a b) -> p a b", a=2),
                                       in1=rowof(l, 0).unsqueeze(1).to_broadcast([P, NT, HEADS]), op=ALU.add))
                dve.tensor_scalar(sdt[:, 5, :, :], sdt[:, 0, :, :], 0.0, None, ALU.max).then_inc(dt_sum, 1)
                dve.wait_ge(dt_ln, l + 1)
                link(dve.tensor_tensor(out=sdt[:, 2, :, :], in0=sdt[:, 5, :, :], in1=sdt[:, 1, :, :], op=ALU.add))
                dve.scalar_tensor_tensor(sdt[:, 3, :, :], sdt[:, 2, :, :], -1.0,
                                         sdt[:, 4, 0, :].unsqueeze(1).to_broadcast([P, NT, HEADS]),
                                         ALU.mult, ALU.mult).then_inc(dt_a, 1)
                dve.wait_ge(a_hi_made, l + 1)
                dve.tensor_tensor(out=a_lo[:, :, :], in0=sdt[:, 3, :, :], in1=a_hi[:, :, :].bitcast(F32),
                                  op=ALU.subtract).then_inc(a_lo_made, 1)

                def blocks(t):
                    return t[:, :, :].rearrange("p h (b c) -> p h b c", b=3)[:, :, 0:3:2, :]

                def softplus(p):
                    z = ps[:, 2 + 2 * (p % 2):4 + 2 * (p % 2), 0:384]
                    dve.wait_ge(sb_ln, 4 * l + p + 1)
                    if 4 * l + p >= 1:
                        dve.wait_ge(sb_lp, 4 * l + p)
                    link(dve.scalar_tensor_tensor(sbp[:, :, :], z, 0.0, sbl[:, :, :], ALU.max, ALU.add))
                    dve.tensor_tensor(out=blocks(sbp), in0=blocks(sbp),
                                      in1=tri_lt[:, :].unsqueeze(1).unsqueeze(1).to_broadcast([P, 2, 2, P]),
                                      op=ALU.mult).then_inc(sb_sp, 1)

                def mask_att(p):
                    dve.wait_ge(sb_exp, 4 * l + p + 1)
                    for a in range(2):
                        b = blocks(sba)[:, a]
                        dve.scalar_tensor_tensor(b, b, 1.0, tri_lt[:, :].unsqueeze(1).to_broadcast([P, 2, P]),
                                                 ALU.min, ALU.mult).then_inc(sb_att, 1)

                def y_lo_out(p):
                    dve.wait_ge(sb_hi, 4 * l + p + 1)
                    dve.tensor_tensor(out=o_lo[:, p, :], in0=ps[:, 6 + p % 2, 0:S],
                                      in1=o_hi[:, p, :].bitcast(F32), op=ALU.subtract).then_inc(sb_lo, 1)

                def conv(n):
                    j = (4, 0, 1, 2, 3)[n]
                    if l == 0 and n == 0:
                        dve.wait_ge(params_in, 48)
                    if n == 0:
                        if l:
                            dve.wait_ge(merged_hi, 4 * l)
                            dve.wait_ge(xs_ps, 4 * l)
                        link(dve.memset(xconv[:, :, 0:CONV - 1], 0.0))
                    feed(UNIT_OF[l, "xbc", j] + 2)
                    dve.wait_ge(out_read_act, out_reader(OUT_NO[l, "xbc", j, 0])[1])
                    for i in range(CONV):
                        for f in (2 * j, 2 * j + 1):
                            w0 = (l * CT + f) * (CONV + 1)
                            src = xconv[:, f, i:i + S]
                            if i == 0:
                                ins = dve.tensor_scalar(xc[:, f, :], src, cw[:, w0:w0 + 1],
                                                        cw[:, w0 + CONV:w0 + CONV + 1], ALU.mult, ALU.add)
                            else:
                                ins = dve.scalar_tensor_tensor(xc[:, f, :], src, cw[:, w0 + i:w0 + i + 1],
                                                               xc[:, f, :], ALU.mult, ALU.add)
                        if i < CONV - 1:
                            link(ins)
                        else:
                            ins.then_inc(conved, 1)

                feed(UNIT_OF[l, "v", 1] + 2)
                softplus(0)
                softplus(1)
                mask_att(0)
                conv(0)
                mask_att(1)
                conv(1)
                softplus(2)
                y_lo_out(0)
                conv(2)
                softplus(3)
                mask_att(2)
                y_lo_out(1)
                conv(3)
                mask_att(3)
                conv(4)
                y_lo_out(2)
                y_lo_out(3)
                feed(UNIT_OF[l, "ga", 0] + 2)
                dve.wait_ge(b_tok, l + 1)
                for g in range(2):
                    dve.tensor_tensor(out=cbm[:, :, g, :], in0=ps[:, 7 - g, P:3 * P].rearrange("p (a c) -> p a c", a=2),
                                      in1=tri_le[:, :].unsqueeze(1).to_broadcast([P, 2, P]),
                                      op=ALU.mult).then_inc(cb_made, 1)
                for r in range(4):
                    t, g = r // 2, r % 2
                    dve.wait_ge(x_tok, 4 * l + r + 1)
                    dve.tensor_tensor(out=xdt[:, t, 512 * g:512 * g + 512].rearrange("p (h d) -> p h d", h=8),
                                      in0=ps[:, 2 + r, :].rearrange("p (h d) -> p h d", h=8),
                                      in1=sdt[:, 2, t, 8 * g:8 * g + 8].unsqueeze(2).to_broadcast([P, 8, HD]),
                                      op=ALU.mult).then_inc(x_dt, 1)
                dve.wait_ge(dt_exp, l + 1)
                dve.wait_ge(x_dt, 4 * l + 2)
                if l:
                    dve.wait_ge(xp_turned, 4 * l)
                dve.tensor_tensor(out=xdte.rearrange("p (h d) -> p h d", h=HEADS),
                                  in0=xdt[:, 0, :].rearrange("p (h d) -> p h d", h=HEADS),
                                  in1=eacum[:, 1, :].unsqueeze(2).to_broadcast([P, HEADS, HD]),
                                  op=ALU.mult).then_inc(st_in, 1)
                feed(UNIT_OF[l, "gb", 0])

                def head_products(c):
                    dve.wait_ge(cb_made, 2 * l + 2)
                    dve.wait_ge(decayed, 2 * l + c + 1)
                    for g in range(2):
                        d = decay[:, 8 * g:8 * g + 8, :]
                        dve.tensor_tensor(out=d, in0=d, in1=cbm[:, c, g, :].unsqueeze(1).to_broadcast([P, 8, P]),
                                          op=ALU.mult).then_inc(m_made, 1)

                def add_y(c):
                    dve.wait_ge(y_skip, 2 * l + c + 1)
                    dve.wait_ge(y_ps, 2 * l + c + 1)
                    dve.tensor_tensor(out=xn[:, c, :], in0=xn[:, c, :],
                                      in1=ps[:, 6:8, :].rearrange("p a b -> p (a b)"), op=ALU.add).then_inc(y_read, 1)

                feed(UNIT_OF[l, "ga", 1] + 2)
                head_products(0)
                feed(UNIT_OF[l, "gb", 1])
                add_y(0)
                dve.wait_ge(yoff_ps, l + 1)
                for g in range(2):
                    dve.tensor_tensor(out=yoff[:, 512 * g:512 * g + 512].rearrange("p (h d) -> p h d", h=8),
                                      in0=ps[:, 2 + g, :].rearrange("p (h d) -> p h d", h=8),
                                      in1=eacum[:, 0, 8 * g:8 * g + 8].unsqueeze(2).to_broadcast([P, 8, HD]),
                                      op=ALU.mult).then_inc(yoff_read, 1)
                feed(UNIT_OF[l, "gb", 2])
                dve.wait_ge(yoff_read, 2 * l + 2)
                dve.wait_ge(y_skip, 2 * l + 2)
                dve.tensor_tensor(out=xn[:, 1, :], in0=xn[:, 1, :], in1=yoff, op=ALU.add).then_inc(yoff_added, 1)
                head_products(1)
                feed(UNIT_OF[l, "gb", 1] + 2)
                dve.wait_ge(yoff_added, l + 1)
                add_y(1)
                for j in range(4):
                    feed(UNIT_OF[l, "z", j] + 2)
                    dve.wait_ge(out_read_act, out_reader(OUT_NO[l, "z", j, 0])[1])
                    dve.wait_ge(y_read, 2 * l + 2)
                    dve.tensor_tensor(out=xn[:, :, 256 * j:256 * j + 256], in0=xn[:, :, 256 * j:256 * j + 256],
                                      in1=zs[:, j % 2, :, :], op=ALU.mult).then_inc(z_mul, 1)
                i = l * NNORM + N_SSD
                for t in range(NT):
                    dve.wait_ge(rstd, 2 * i + t + 1)
                    dve.tensor_tensor(out=xn[:, t, :].rearrange("p (g f) -> p g f", g=2),
                                      in0=xn[:, t, :].rearrange("p (g f) -> p g f", g=2),
                                      in1=rs[:, 4 * i + 2 * t:4 * i + 2 * t + 2].unsqueeze(2)
                                      .to_broadcast([P, 2, D // 2]), op=ALU.mult).then_inc(normed, 1)

                def gated_sb(j, part):
                    if part == 0:
                        dve.wait_ge(half_unit, 4 * l + j + 1)
                    else:
                        dve.wait_ge(unit_used, UNIT_OF[l, "sbo", j] + 1)
                    o = ps[:, OUT_NO[l, "sbo", j, part] % 2, :]
                    f = 4 * j + 2 * part
                    dve.scalar_tensor_tensor(merged[:, f:f + 2, :], gb[:, f:f + 2, :], 1.0,
                                             o.rearrange("p (a b) -> p a b", a=2), ALU.add,
                                             ALU.mult).then_inc(out_read_dve, 1)

                gated_sb(0, 0)
                gated_sb(0, 1)
                feed(UNIT_OF[l, "ssdo", 0])
                turn_lo(l, N_SSD, m_hi, m_lo)
                gated_sb(1, 0)
                feed(UNIT_OF[l, "ssdo", 1])
                gated_sb(1, 1)
                normalise(l, N_MEM, xtok)

                def merged_lo_half(j):
                    dve.wait_ge(merged_hi, 4 * l + j + 1)
                    dve.scalar_tensor_tensor(u_lo[:, 2 * j:2 * j + 2, :], merged[:, 2 * j:2 * j + 2, :], 0.5,
                                             u_hi[:, 2 * j:2 * j + 2, :].bitcast(F32), ALU.mult,
                                             ALU.subtract).then_inc(merged_lo, 1)

                for j in range(4):
                    o = result(l, "ssdo", j)
                    part = zs[:, 0, :, :]
                    if j == 0:
                        dve.wait_ge(z_mul, 4 * l + 4)
                    else:
                        dve.wait_ge(merged_sum, 4 * l + j)
                    dve.scalar_tensor_tensor(part, ga[:, 2 * j:2 * j + 2, :], 1.0,
                                             o.rearrange("p (a b) -> p a b", a=2), ALU.add,
                                             ALU.mult).then_inc(out_read_dve, 1)
                    dve.wait_ge(out_read_dve, out_reader(OUT_NO[l, "ssdo", j, 0])[1])
                    dve.tensor_tensor(out=merged[:, 2 * j:2 * j + 2, :], in0=merged[:, 2 * j:2 * j + 2, :],
                                      in1=part, op=ALU.add).then_inc(merged_sum, 1)
                    if j < 3:
                        feed(UNIT_OF[l, "ssdo", j] + 3)
                    if j:
                        merged_lo_half(j - 1)
                merged_lo_half(3)
                turn_lo(l, N_MEM, m_hi, m_lo)
                for j in range(4):
                    o = result(l, "wout", j)
                    dve.tensor_tensor(out=h[:, :, 256 * j:256 * j + 256], in0=h[:, :, 256 * j:256 * j + 256],
                                      in1=o.rearrange("p (a b) -> p a b", a=2), op=ALU.add)\
                        .then_inc(out_read_dve, 1)
                feed(UNIT_OF[l, "xk", 0] + 2)
                normalise(l, N_XA, h)
                feed(UNIT_OF[l, "xv", 1])
                turn_lo(l, N_XA, u_hi, u_lo)
                feed(UNIT_OF[l, "xq", 1] + 2)
                for a in range(XH):
                    dve.wait_ge(xs_ps, 4 * l + a + 1)
                    link(dve.tensor_reduce(xmx[:, 0, a, :], ps[:, 2 + a, :].rearrange("p (t m) -> p t m", t=NT),
                                           AX.X, ALU.max))
                    dve.tensor_scalar(xmx[:, 1, a, :], xmx[:, 0, a, :], -XSCALE, None, ALU.mult).then_inc(xs_max, 1)
                for a in range(XH):
                    dve.wait_ge(xs_exp, 8 * l + 2 * a + 2)
                    link(dve.reciprocal(xmx[:, 3, a, :], xmx[:, 2, a, :]))
                    for t in range(NT):
                        dve.tensor_scalar(prob[:, 2 * a + t, :], prob[:, 2 * a + t, :], xmx[:, 3, a, t:t + 1], None,
                                          ALU.mult).then_inc(xs_p, 1)
                for a in range(XH):
                    dve.wait_ge(xo_hi, 4 * l + a + 1)
                    dve.tensor_tensor(out=o_lo[:, a, :], in0=ps[:, 6 + a % 2, 0:S],
                                      in1=o_hi[:, a, :].bitcast(F32), op=ALU.subtract).then_inc(xo_lo, 1)
                for j in range(2):
                    for part in range(2):
                        feed(UNIT_OF[l, "xo", j] + 2 - j)
                        if part:
                            dve.wait_ge(unit_used, UNIT_OF[l, "xo", j] + 1)
                        else:
                            dve.wait_ge(half_unit, 4 * l + 2 + j + 1)
                        o = ps[:, OUT_NO[l, "xo", j, part] % 2, :]
                        dve.tensor_tensor(out=h[:, part, 512 * j:512 * j + 512], in0=h[:, part, 512 * j:512 * j + 512],
                                          in1=o, op=ALU.add).then_inc(out_read_dve, 1)
                if l == DEPTH - 1:
                    dve.memset(selT[:, :].bitcast(F32), 0.0)
                    dve.memset(wslot[:, :], 0.0)
                    for v in (rank2, mask2):
                        link(dve.memset(v[:, :, 2 * NE:], 0.0))
                    dve.memset(comb2[:, :, 2 * NE:], 0.0).then_inc(e_add, 1)
                normalise(l, N_FFN, h)
                turn_lo(l, N_FFN, u_hi, u_lo)
                if l == 0:
                    for c in range(CH):
                        for f in range(2):
                            n = 2 * c + f
                            feed(FFN0 + up_unit(c) + 2)
                            if n >= 2:
                                dve.wait_ge(f_hi, n - 1)
                                dve.wait_ge(f_lo, n - 1)
                            dve.wait_ge(f_silu, n + 1)
                            dve.tensor_tensor(out=act_f[:, f, :], in0=sg[:, f, :], in1=ps[:, n % 4, S:2 * S],
                                              op=ALU.mult).then_inc(f_act, 1)
                        for f in range(2):
                            dve.wait_ge(f_hi, 2 * c + f + 1)
                            dve.tensor_tensor(out=hT_lo[:, c % 2, f, :], in0=act_f[:, f, :],
                                              in1=hT_hi[:, c % 2, f, :].bitcast(F32), op=ALU.subtract).then_inc(f_lo, 1)
                    feed(LAYER1 + 1)
                    for t in range(NT):
                        if t == 0:
                            dve.wait_ge(ffn_half, 1)
                        else:
                            dve.wait_ge(unit_used, LAYER1)
                        for a in range(2):
                            dve.tensor_tensor(out=h[:, t, 512 * a:512 * a + 512], in0=h[:, t, 512 * a:512 * a + 512],
                                              in1=ps[:, 4 + 2 * t + a, :], op=ALU.add).then_inc(h_ffn, 1)

            def select(column):
                for t in range(NT):
                    dve.tensor_scalar(sel[:, t, :], iota[:, :], rank2[:, t, column],
                                      mask2[:, t, column], ALU.is_equal, ALU.mult).then_inc(sel_made, 1)


            dve.wait_ge(logitT_ps, 1)
            dve.tensor_copy(by_expert, ps[0:NE, 6, 0:S]).then_inc(logitT_out, 1)
            dve.wait_ge(consts, 10)
            dve.wait_ge(r_ps, 1)
            logit, left, eq, best, one0, one1, mask, rank = (rt[:, i] for i in range(8))
            frst = first[:, :].unsqueeze(1).to_broadcast([P, NT, NE])

            def wide(v):
                return v.unsqueeze(2).to_broadcast([P, NT, NE])

            link(dve.tensor_copy(logit, ps[:, 6, 0:NT * NE].rearrange("p (t e) -> p t e", t=NT)))
            link(dve.tensor_copy(left, logit))
            for i, one in enumerate((one0, one1)):
                link(dve.tensor_reduce(rt1[:, i, :], left, AX.X, ALU.max))
                link(dve.tensor_tensor(out=eq, in0=left, in1=wide(rt1[:, i, :]), op=ALU.is_equal))
                link(dve.tensor_tensor(out=best, in0=eq, in1=frst, op=ALU.mult))
                link(dve.tensor_reduce(rt1[:, 2, :], best, AX.X, ALU.max))
                link(dve.tensor_tensor(out=one, in0=best, in1=wide(rt1[:, 2, :]), op=ALU.is_equal))
                if i == 0:
                    link(dve.scalar_tensor_tensor(left, one, -3.0e38, logit, ALU.mult, ALU.add))
            link(dve.tensor_tensor(out=rt1[:, 3, :], in0=rt1[:, 1, :], in1=rt1[:, 0, :], op=ALU.subtract))
            dve.tensor_tensor(out=mask, in0=one0, in1=one1, op=ALU.add).then_inc(r_mask, 1)
            dve.wait_ge(r_exp, 1)
            link(dve.tensor_scalar(rt1[:, 5, :], rt1[:, 4, :], 1.0, None, ALU.add))
            link(dve.reciprocal(rt1[:, 6, :], rt1[:, 5, :]))
            link(dve.tensor_tensor(out=rt1[:, 7, :], in0=rt1[:, 4, :], in1=rt1[:, 6, :], op=ALU.mult))
            link(dve.tensor_tensor(out=one0, in0=one0, in1=wide(rt1[:, 6, :]), op=ALU.mult))
            link(dve.tensor_tensor(out=one1, in0=one1, in1=wide(rt1[:, 7, :]), op=ALU.mult))
            for i in range(2):
                e = slice(NE * i, NE * i + NE)
                dve.tensor_tensor(out=comb2[:, :, e], in0=one0, in1=one1, op=ALU.add).then_inc(r_twice, 1)
                dve.tensor_copy(mask2[:, :, e], mask).then_inc(r_twice, 1)
            dve.wait_ge(r_twice, 4)
            dve.wait_ge(r_rank, 1)
            link(dve.tensor_copy(rank2[:, :, 0:NE], ps[:, 7, 0:16].rearrange("p (t e) -> p t e", t=NT)))
            select(slice(0, 1))
            dve.wait_ge(r_count, 1)
            link(dve.tensor_reduce(visits[:, 0:1], ps[:, 5, 0:NE], AX.X, ALU.max))
            link(dve.tensor_scalar(visits[:, 1:2], visits[:, 0:1], 128.5, float(NE), ALU.is_gt, ALU.mult))
            link(dve.tensor_scalar(visits[:, 2:3], visits[:, 1:2], float(NE), None, ALU.add))
            dve.tensor_copy(visits_i[:, :], visits[:, 2:3]).then_inc(r_done, 1)
            link(dve.tensor_scalar(rank2[:, :, NE:2 * NE], rank2[:, :, 0:NE], -128.0, None, ALU.add))
            feed(MOE0 + 1)

            def gathered(count, r):
                dve.wait_ge(ue_hi_out, count)
                dve.tensor_tensor(out=ue_lo[:, 4 * r:4 * r + 4, :],
                                  in0=ps[:, 6 + r, :].rearrange("p (a b) -> p a b", a=4),
                                  in1=ue_hi[:, 4 * r:4 * r + 4, :].bitcast(F32),
                                  op=ALU.subtract).then_inc(ue_lo_out, 1)

            def y_half(count):
                dve.wait_ge(e_yhi, count)
                dve.scalar_tensor_tensor(y_lo, ps[:, 4:6, :].rearrange("p a b -> p (a b)"), wslot[:, 0:1],
                                         y_hi.bitcast(F32), ALU.mult, ALU.subtract).then_inc(e_ylo, 1)

            def add_y(count, i):
                dve.wait_ge(e_sc, count)
                c = slice(512 * (i % 2), 512 * (i % 2) + 512)
                dve.tensor_tensor(out=h[:, i // 2, c], in0=h[:, i // 2, c], in1=ps[:, 6 + i % 2, :],
                                  op=ALU.add).then_inc(e_add, 1)

            dve.wait_ge(r_done, 1)
            n_visits = dve.value_load(visits_i[0:1, 0:1], min_val=NE, max_val=2 * NE)
            for r in range(2):
                gathered(r + 1, r)
            y_half(1)
            feed(MOE0 + AHEAD - 1)
            with dve.Fori(0, n_visits) as n:
                slots = [dve.snap((n * EU + (RAW + s)) % RAW_E) for s in range(RAW_E)]

                def split_e(j):
                    dve.wait_ge(hi_made, n * EU + (MOE0 + j + 1))
                    dve.tensor_tensor(out=wlo[:, (MOE0 + j) % HL, :], in0=raw_e[:, bass.ds(slots[j % RAW_E], 1), :],
                                      in1=whi[:, (MOE0 + j) % HL, :].bitcast(F32),
                                      op=ALU.subtract).then_inc(lo_made, 1)

                for c in range(CH):
                    if c:
                        split_e(3 * c + 2)
                    dve.wait_ge(e_silu, n * CH + (c + 1))
                    if c >= 2:
                        dve.wait_ge(e_turn, n * CH + (c - 1))
                    dve.tensor_tensor(out=act_f[:, c % 2, :], in0=sg[:, c % 2, :], in1=ps[:, c % 2, 256:512],
                                      op=ALU.mult).then_inc(e_act, 1)
                    if c == 0:
                        add_y(n * 4 + 1, 0)
                        add_y(n * 4 + 2, 1)
                    if 3 * c + 3 < EU:
                        split_e(3 * c + 3)
                    if c and 3 * c + 4 < EU:
                        split_e(3 * c + 4)
                    if c == CH - 1:
                        for r in range(2):
                            gathered(2 * n + (r + 3), r)
                    dve.wait_ge(e_hi, n * CH + (c + 1))
                    dve.tensor_tensor(out=hT_lo[:, c % 2, 0, :], in0=ps[:, 2 + c % 2, 0:256],
                                      in1=hT_hi[:, c % 2, 0, :].bitcast(F32), op=ALU.subtract).then_inc(e_lo, 1)
                    if c == 0:
                        add_y(n * 4 + 3, 2)
                        add_y(n * 4 + 4, 3)
                        split_e(4)
                    if c == 2:
                        dve.wait_ge(w_ps, n + 1)
                        select(bass.ds(n + 1, 1))
                split_e(EU)
                split_e(EU + 1)
                y_half(n + 2)
                split_e(EU + 2)
            for i in range(4):
                add_y(n_visits * 4 + (i + 1), i)
            i = DEPTH * NNORM
            dve.wait_ge(frow_in, 16)
            for t in range(NT):
                dve.wait_ge(rstd, 2 * i + t + 1)
                dve.scalar_tensor_tensor(xn[:, t, :], h[:, t, :], rs[:, 4 * i + t:4 * i + t + 1], frow,
                                         ALU.mult, ALU.mult).then_inc(final_made, 1)

        @block.tensor
        def _(pe):
            def three(o, a_hi, a_lo, b_hi, b_lo, start, stop):
                pe.matmul(o, a_hi, b_hi, start=start, stop=False)
                pe.matmul(o, a_lo, b_hi, start=False, stop=False)
                return pe.matmul(o, a_hi, b_lo, start=False, stop=stop)

            def w(buf, u, k, c, n, width):
                return buf[:, u % HL, k * width + c:k * width + c + n]

            def begin(l, name, j, part=0):
                i = OUT_NO[l, name, j, part]
                if part == 0:
                    pe.wait_ge(lo_made, UNIT_OF[l, name, j] + 1)
                if i >= 2:
                    dve, count = out_reader(i - 2)
                    pe.wait_ge(out_read_dve if dve else out_read_act, count)
                return ps[:, i % 2, :]

            def by_token(l, name, j, a_hi, a_lo, ready=None):
                u, o = UNIT_OF[l, name, j], begin(l, name, j)
                for t in range(NT):
                    for k in range(KD):
                        if ready and t == 0:
                            pe.wait_ge(*ready(k))
                        ins = three(o[:, 256 * t:256 * t + 256], a_hi[:, k, P * t:P * t + P], a_lo[:, k, P * t:P * t + P],
                                    w(whi, u, k, 0, 256, 256), w(wlo, u, k, 0, 256, 256), k == 0, k == KD - 1)
                ins.then_inc(unit_used, 1)

            def by_feature(l, name, j, a_hi, a_lo, ready=None):
                u, o = UNIT_OF[l, name, j], begin(l, name, j)
                for f in range(2):
                    for k in range(KD):
                        if ready and f == 0:
                            pe.wait_ge(*ready(k))
                        ins = three(o[:, S * f:S * f + S], w(whi, u, k, P * f, P, 256), w(wlo, u, k, P * f, P, 256),
                                    a_hi[:, k, :], a_lo[:, k, :], k == 0, k == KD - 1)
                ins.then_inc(unit_used, 1)

            def turn(l, n, free_sem, free):
                i = l * NNORM + n
                pe.wait_ge(free_sem, free)
                for t in range(NT):
                    pe.wait_ge(normed, 2 * i + t + 1)
                    for r in range(4):
                        for k in range(2):
                            f = 2 * r + k
                            ins = pe.transpose(ps[:, 2 + r, S * k + P * t:S * k + P * t + P],
                                               xn[:, t, P * f:P * f + P], ident[:, :])
                        if t:
                            ins.then_inc(turned, 1)

            def turned_tile(l, n):
                return lambda k: (turned_lo, 8 * (l * NNORM + n) + k + 1)

            pe.wait_ge(consts, 10)
            for l in range(DEPTH):
                if l == 0:
                    turn(l, N_MIX, consts, 10)
                else:
                    turn(l, N_MIX, h_ffn, 4)
                pe.wait_ge(small_lo, l + 1)
                for k in range(KD):
                    c = slice(16 * k, 16 * k + 16)
                    pe.wait_ge(*turned_tile(l, N_MIX)(k))
                    ins = three(ps[0:HEADS, 7, 0:S], wdt_hi[:, c], wdt_lo[:, c], u_hi[:, k, :], u_lo[:, k, :],
                                k == 0, k == KD - 1)
                ins.then_inc(dtT_ps, 1)
                by_feature(l, "q", 0, u_hi, u_lo)
                by_feature(l, "q", 1, u_hi, u_lo)
                pe.wait_ge(dtT_out, l + 1)
                for t in range(NT):
                    ins = pe.transpose(ps[:, 7, HEADS * t:HEADS * t + HEADS], by_head[:, P * t:P * t + P],
                                       ident[0:HEADS, 0:HEADS])
                ins.then_inc(dt_ps, 1)
                for j in range(2):
                    by_feature(l, "k", j, u_hi, u_lo)
                pe.wait_ge(dt_a, l + 1)
                pe.matmul(ps[:, 7, 64:80], tri_le[:, :], sdt[:, 3, 1, :], start=True, stop=True)
                pe.matmul(ps[:, 7, 80:96], tri_gt[:, :], sdt[:, 3, 0, :], start=True, stop=True).then_inc(dt_cum, 1)
                for j in range(2):
                    by_token(l, "v", j, u_hi, u_lo)

                def scores(p):
                    pe.wait_ge(out_read_act, out_reader(OUT_NO[l, "k", 1, 0])[1])
                    if p >= 2:
                        pe.wait_ge(sb_exp, 4 * l + p - 1)
                    elif l == 0:
                        pe.wait_ge(turned_lo, 8)
                    for a in range(2):
                        o = ps[:, 2 + 2 * (p % 2) + a, :]
                        r = slice(HD * a, HD * a + HD)
                        pe.matmul(o[:, 0:S], qk[r, 4 + p, 0:P], qk[r, p, 0:S], start=True, stop=False,
                                  skip_group_check=True)
                        ins = pe.matmul(o[:, S:S + P], qk[r, 4 + p, P:S], qk[r, p, P:S], start=False, stop=False,
                                        skip_group_check=True)
                    ins.then_inc(sb_z, 1)

                def log_between(p):
                    pe.wait_ge(sb_sp, 4 * l + p + 1)
                    for a in range(2):
                        o = ps[:, 2 + 2 * (p % 2) + a, :]
                        pe.matmul(o[:, 0:S], neg_ge[:, :], sbp[:, a, 0:S], start=False, stop=False,
                                  skip_group_check=True)
                        pe.matmul(o[:, P:S], neg_one[:, :], sbp[:, a, S:S + P], start=False, stop=False,
                                  skip_group_check=True)
                        ins = pe.matmul(o[:, S:S + P], neg_ge[:, :], sbp[:, a, S:S + P], start=False, stop=True,
                                        skip_group_check=True)
                    ins.then_inc(sb_lp, 1)

                def attend(p):
                    pe.wait_ge(sb_att, 2 * (4 * l + p + 1))
                    if p == 0:
                        pe.wait_ge(out_read_act, out_reader(OUT_NO[l, "v", 1, 0])[1])
                        pe.wait_ge(dt_exp, l + 1)
                    if p >= 2:
                        pe.wait_ge(sb_lo, 4 * l + p - 1)
                    for a in range(2):
                        f = P * p + HD * a
                        o = ps[HD * a:HD * a + HD, 6 + p % 2, :]
                        pe.matmul(o[:, 0:S], va[:, 0, f:f + HD], sba[:, a, 0:S], start=True, stop=False,
                                  skip_group_check=True)
                        ins = pe.matmul(o[:, P:S], va[:, 1, f:f + HD], sba[:, a, S:S + P], start=False, stop=True,
                                        skip_group_check=True)
                    ins.then_inc(sb_y, 1)

                scores(0)
                scores(1)
                by_feature(l, "xbc", 4, u_hi, u_lo)
                log_between(0)
                by_feature(l, "xbc", 0, u_hi, u_lo)
                attend(0)
                scores(2)
                log_between(1)
                by_feature(l, "xbc", 1, u_hi, u_lo)
                attend(1)
                scores(3)
                by_feature(l, "xbc", 2, u_hi, u_lo)
                log_between(2)
                by_feature(l, "xbc", 3, u_hi, u_lo)
                attend(2)
                log_between(3)
                by_feature(l, "ga", 0, u_hi, u_lo)
                attend(3)

                by_feature(l, "ga", 1, u_hi, u_lo)
                pe.wait_ge(silued, 5 * l + 1)
                pe.wait_ge(sb_lo, 4 * l + 4)
                for g in range(2):
                    for c in range(2):
                        r, t = slice(64 * g, 64 * g + 64), slice(P * c, P * c + P)
                        pe.matmul(ps[:, 7 - g, P * (c + 1):P * (c + 1) + P], xc[r, 8, t], xc[r, 9, t],
                                  start=True, stop=True)
                pe.transpose(ps[:, 6, 0:P], xc[:, 8, 0:P], ident[:, :]).then_inc(b_turned, 1)
                pe.wait_ge(silued, 5 * l + 5)
                for r in range(4):
                    t, g = r // 2, r % 2
                    for k in range(4):
                        ins = pe.transpose(ps[:, 2 + r, P * k:P * k + P], xc[:, 4 * g + k, P * t:P * t + P], ident[:, :])
                    ins.then_inc(x_turned, 1)
                by_feature(l, "ga", 2, u_hi, u_lo)

                def log_decays(c):
                    pe.wait_ge(a_tri, 4 * l + 2 * c + 2)
                    if c == 0:
                        pe.wait_ge(x_dt, 4 * l + 4)
                    else:
                        pe.wait_ge(yoff_read, 2 * l + 2)
                    for b in range(4):
                        pe.matmul(ps[:, 2 + b, :], tri_gt_r[:, :], atri_hi[:, 4 * b:4 * b + 4, :], start=True, stop=False)
                        ins = pe.matmul(ps[:, 2 + b, :], tri_gt_r[:, :], atri_lo[:, 4 * b:4 * b + 4, :],
                                        start=False, stop=True)
                    ins.then_inc(seg, 1)

                def y_within(c):
                    pe.wait_ge(m_made, 4 * l + 2 * c + 2)
                    if c == 0:
                        pe.wait_ge(b_tok, l + 1)
                        pe.wait_ge(cb_made, 2 * l + 2)
                        pe.wait_ge(x_dt, 4 * l + 4)
                    else:
                        pe.wait_ge(y_read, 2 * l + 1)
                    for a in range(HEADS):
                        ins = pe.matmul(ps[:, 6 + a // 8, HD * (a % 8):HD * (a % 8) + HD], decay[:, a, :],
                                        xdt[:, c, HD * a:HD * a + HD], start=True, stop=True)
                    ins.then_inc(y_ps, 1)

                pe.wait_ge(tri_r, 1)
                log_decays(0)
                by_feature(l, "ga", 3, u_hi, u_lo)
                pe.wait_ge(st_in, l + 1)
                pe.wait_ge(decayed, 2 * l + 1)
                pe.wait_ge(b_tok, l + 1)
                for g in range(2):
                    ins = pe.matmul(ps[64 * g:64 * g + 64, 2, :], btok[:, 64 * g:64 * g + 64],
                                    xdte[:, 512 * g:512 * g + 512], start=True, stop=True)
                ins.then_inc(st_ps, 1)
                by_feature(l, "gb", 0, u_hi, u_lo)
                y_within(0)
                pe.wait_ge(st_out, l + 1)
                for g in range(2):
                    r = slice(64 * g, 64 * g + 64)
                    ins = pe.matmul(ps[:, 2 + g, :], xc[r, 9, P:S], prev[r, :], start=True, stop=True)
                ins.then_inc(yoff_ps, 1)
                by_feature(l, "gb", 1, u_hi, u_lo)
                log_decays(1)
                by_feature(l, "gb", 2, u_hi, u_lo)
                y_within(1)
                by_feature(l, "gb", 3, u_hi, u_lo)
                for j in range(4):
                    by_token(l, "z", j, u_hi, u_lo)

                for j in range(2):
                    u = UNIT_OF[l, "sbo", j]
                    pe.wait_ge(sb_lo, 4 * l + 4)
                    for part in range(2):
                        o = begin(l, "sbo", j, part)
                        for f in range(2):
                            for k in range(4):
                                c = P * (2 * part + f)
                                ins = three(o[:, S * f:S * f + S], w(whi, u, k, c, P, 512), w(wlo, u, k, c, P, 512),
                                            o_hi[:, k, :], o_lo[:, k, :], k == 0, k == 3)
                        if part:
                            ins.then_inc(unit_used, 1)
                        else:
                            ins.then_inc(half_unit, 1)
                    if j == 0:
                        turn(l, N_SSD, decayed, 2 * l + 2)
                for j in range(4):
                    by_feature(l, "ssdo", j, m_hi, m_lo, None if j else turned_tile(l, N_SSD))
                turn(l, N_MEM, turned_lo, 8 * (l * NNORM + N_MEM))
                for j in range(4):
                    by_token(l, "wout", j, u_hi, u_lo, None if j else lambda k: (merged_lo, 4 * l + k // 2 + 1))
                for j in range(2):
                    by_feature(l, "xk", j, m_hi, m_lo, None if j else turned_tile(l, N_MEM))
                turn(l, N_XA, turned_lo, 8 * (l * NNORM + N_XA))
                for j in range(2):
                    by_token(l, "xv", j, m_hi, m_lo)
                for j in range(2):
                    by_feature(l, "xq", j, u_hi, u_lo, None if j else turned_tile(l, N_XA))
                pe.wait_ge(out_read_act, out_reader(OUT_NO[l, "xq", 1, 0])[1])
                for a in range(XH):
                    for t in range(NT):
                        ins = pe.matmul(ps[:, 2 + a, S * t:S * t + S], qx[:, a, P * t:P * t + P], kx[:, a, :],
                                        start=True, stop=True)
                    ins.then_inc(xs_ps, 1)
                for a in range(XH + 1):
                    if a < XH:
                        pe.wait_ge(xs_p, 8 * l + 2 * a + 2)
                        for m in range(2):
                            for t in range(NT):
                                ins = pe.transpose(ps[:, 2 + a, S * m + P * t:S * m + P * t + P],
                                                   prob[:, 2 * a + t, P * m:P * m + P], ident[:, :])
                        ins.then_inc(xp_turned, 1)
                    if a:
                        b = a - 1
                        pe.wait_ge(xp_out, 4 * l + b + 1)
                        if b >= 2:
                            pe.wait_ge(xo_lo, 4 * l + b - 1)
                        else:
                            pe.wait_ge(y_read, 2 * l + 2)
                        for m in range(2):
                            ins = pe.matmul(ps[:, 6 + b % 2, 0:S], vx[:, m, P * b:P * b + P], pT[:, 2 * (b % 2) + m, :],
                                            start=(m == 0), stop=(m == 1))
                        ins.then_inc(xo_ps, 1)
                pe.wait_ge(xo_lo, 4 * l + 4)
                for j in range(2):
                    u = UNIT_OF[l, "xo", j]
                    for part in range(2):
                        o = begin(l, "xo", j, part)
                        for k in range(4):
                            ins = three(o, o_hi[:, k, P * part:P * part + P], o_lo[:, k, P * part:P * part + P],
                                        w(whi, u, k, 0, 512, 512), w(wlo, u, k, 0, 512, 512), k == 0, k == 3)
                        if part:
                            ins.then_inc(unit_used, 1)
                        else:
                            ins.then_inc(half_unit, 1)
                turn(l, N_FFN, turned_lo, 8 * (l * NNORM + N_FFN))
                if l == 0:
                    pe.wait_ge(out_read_dve, sum(o[0] == 0 and o[1] in BY_DVE for o in OUTS))

                    def gate_up(unit, c, which, first_use, slot):
                        pe.wait_ge(lo_made, unit + 1)
                        for f in range(2):
                            if which == 0 and not first_use:
                                pe.wait_ge(f_act, first_f_act(c) + f)
                            for k in range(KD):
                                if which == 0 and first_use and c == 0 and f == 0:
                                    pe.wait_ge(*turned_tile(0, N_FFN)(k))
                                a = k * 256 + P * f
                                ins = three(ps[:, bank_of(c, f), S * which:S * which + S],
                                            whi[:, slot, a:a + P], wlo[:, slot, a:a + P],
                                            u_hi[:, k, :], u_lo[:, k, :], k == 0, k == KD - 1)
                            if which:
                                ins.then_inc(unit_used if f else gu_ps, 1)
                            elif f:
                                ins.then_inc(unit_used, 1)

                    chunk_no = [0]

                    def bank_of(c, f):
                        return (2 * chunk_no[0] + f) % 4

                    def first_f_act(c):
                        return 2 * c - 3

                    def down(unit, c, parity, slot, start, stop):
                        pe.wait_ge(lo_made, unit + 1)
                        pe.wait_ge(f_lo, 2 * c + 2)
                        for t in range(NT):
                            for a in range(2):
                                for k in range(2):
                                    b = D * k + 512 * a
                                    ins = three(ps[:, 4 + 2 * t + a, :], hT_hi[:, parity, k, P * t:P * t + P],
                                                hT_lo[:, parity, k, P * t:P * t + P], whi[:, slot, b:b + 512],
                                                wlo[:, slot, b:b + 512], start and k == 0, stop and k == 1)
                            if stop and t == 0:
                                ins.then_inc(ffn_half, 1)
                        return ins

                    gate_up(FFN0, 0, 0, True, FFN0 % HL)
                    gate_up(FFN0 + 1, 0, 1, True, (FFN0 + 1) % HL)
                    for c in range(2):
                        chunk_no[0] = c + 1
                        gate_up(FFN0 + 3 * c + 2, c + 1, 0, c == 0, (FFN0 + 2) % HL)
                        gate_up(FFN0 + 3 * c + 3, c + 1, 1, c == 0, (FFN0 + 3) % HL)
                        down(FFN0 + 3 * c + 4, c, c % 2, (FFN0 + 4) % HL, c == 0, False).then_inc(unit_used, 1)
                    with pe.Fori(1, CH // 2) as i:
                        for half_ in range(2):
                            c = i * 2 + half_
                            chunk_no[0] = half_ + 1
                            gate_up(i * 6 + (FFN0 + 3 * half_ + 2), i * 2 + (half_ + 1), 0, False, (FFN0 + 2) % HL)
                            gate_up(i * 6 + (FFN0 + 3 * half_ + 3), i * 2 + (half_ + 1), 1, False, (FFN0 + 3) % HL)
                            down(i * 6 + (FFN0 + 3 * half_ + 4), c, half_, (FFN0 + 4) % HL, False, False)\
                                .then_inc(unit_used, 1)
                    ins = down(FFN0 + EU - 1, CH - 1, 0, (FFN0 + EU - 1) % HL, False, True)
                    ins.then_inc(unit_used, 1)

            pe.wait_ge(wr_lo_made, 1)
            pe.wait_ge(xo_lo, 8)
            for k in range(KD):
                c = slice(NE * k, NE * k + NE)
                pe.wait_ge(*turned_tile(DEPTH - 1, N_FFN)(k))
                ins = three(ps[0:NE, 6, 0:S], wr_hi[:, c], wr_lo[:, c], u_hi[:, k, :], u_lo[:, k, :],
                            k == 0, k == KD - 1)
            ins.then_inc(logitT_ps, 1)
            pe.wait_ge(logitT_out, 1)
            for t in range(NT):
                ins = pe.transpose(ps[:, 6, NE * t:NE * t + NE], by_expert[:, P * t:P * t + P], ident[0:NE, 0:NE])
            ins.then_inc(r_ps, 1)
            pe.wait_ge(r_mask, 1)
            mask = rt[:, 6]
            pe.matmul(ps[:, 7, 0:NE], tri_lt[:, :], mask[:, 0, :], start=True, stop=True)
            pe.matmul(ps[:, 7, NE:2 * NE], tri_lt[:, :], mask[:, 1, :], start=True, stop=False)
            pe.matmul(ps[:, 7, NE:2 * NE], one[:, :], mask[:, 0, :], start=False, stop=True).then_inc(r_rank, 1)
            pe.matmul(ps[:, 5, 0:NE], one[:, :], mask[:, 0, :], start=True, stop=False)
            pe.matmul(ps[:, 5, 0:NE], one[:, :], mask[:, 1, :], start=False, stop=True).then_inc(r_count, 1)

            def gather(selected):
                pe.wait_ge(sel_made, selected)
                for r in range(2):
                    for k in range(4):
                        f = P * (4 * r + k)
                        o = ps[:, 6 + r, P * k:P * k + P]
                        for t in range(NT):
                            pe.matmul(o, mt_hi[:, t, f:f + P], sel[:, t, :], start=(t == 0), stop=False)
                            ins = pe.matmul(o, mt_lo[:, t, f:f + P], sel[:, t, :], start=False, stop=(t == 1))
                    ins.then_inc(ue_ps, 1)

            def scatter(i):
                t, a = i // 2, i % 2
                o = ps[:, 6 + a, :]
                pe.matmul(o, selT[:, P * t:P * t + P], y_hi[:, 512 * a:512 * a + 512], start=True, stop=False)
                pe.matmul(o, selT[:, P * t:P * t + P], y_lo[:, 512 * a:512 * a + 512], start=False, stop=True)\
                    .then_inc(e_sc, 1)

            pe.wait_ge(ut_lo, NT)
            gather(2)
            pe.wait_ge(r_done, 1)
            n_visits = pe.value_load(visits_i[0:1, 0:1], min_val=NE, max_val=2 * NE)
            with pe.Fori(0, n_visits) as n:
                def gate_up_e(chunk, unit, j, par, which, wait_bank):
                    pe.wait_ge(lo_made, n * EU + (unit + 1))
                    if wait_bank:
                        pe.wait_ge(e_act, n * CH + (chunk - 1))
                    for k in range(KD):
                        ins = three(ps[:, par, 256 * which:256 * which + 256], ue_hi[:, k, :], ue_lo[:, k, :],
                                    w(whi, MOE0 + j, k, 0, 256, 256), w(wlo, MOE0 + j, k, 0, 256, 256),
                                    k == 0, k == KD - 1)
                    ins.then_inc(unit_used, 1)

                def turn_e(chunk, par):
                    pe.wait_ge(e_act, n * CH + (chunk + 1))
                    for f in range(2):
                        ins = pe.transpose(ps[:, 2 + par, P * f:P * f + P], act_f[:, par, P * f:P * f + P], ident[:, :])
                    ins.then_inc(e_turn, 1)

                def down_e(chunk, unit, j, par, start, stop):
                    pe.wait_ge(lo_made, n * EU + (unit + 1))
                    pe.wait_ge(e_lo, n * CH + (chunk + 1))
                    for a in range(2):
                        for k in range(2):
                            ins = three(ps[:, 4 + a, :], hT_hi[:, par, 0, P * k:P * k + P], hT_lo[:, par, 0, P * k:P * k + P],
                                        w(whi, MOE0 + j, k, 512 * a, 512, D), w(wlo, MOE0 + j, k, 512 * a, 512, D),
                                        start and k == 0, stop and k == 1)
                    ins.then_inc(unit_used, 1)
                    return ins

                def steps(i, c, before_up=None, before_down=None, start=False):
                    gate_up_e(i * 2 + (c + 1), i * 6 + (MOE0 + 3 * c + 2), 2, (c + 1) % 2, 0, not start or c)
                    turn_e(i * 2 + c, c)
                    if before_up:
                        before_up()
                    gate_up_e(i * 2 + (c + 1), i * 6 + (MOE0 + 3 * c + 3), 0, (c + 1) % 2, 1, False)
                    if before_down:
                        before_down()
                    down_e(i * 2 + c, i * 6 + (MOE0 + 3 * c + 4), 1, c, start and c == 0, False)

                def scatter_rest():
                    for i in range(2, 4):
                        pe.wait_ge(e_add, n * 4 + i)
                        scatter(i)

                def slots_of_this():
                    pe.wait_ge(e_add, n * 4 + 5)
                    for t in range(NT):
                        ins = pe.transpose(ps[:, 6, P * t:P * t + P], sel[:, t, :].bitcast(F32), ident[:, :])
                    ins.then_inc(selT_ps, 1)
                    for t in range(NT):
                        ins = pe.matmul(ps[:, 7, 0:1], sel[:, t, :].bitcast(F32), comb2[:, t, bass.ds(n, 1)],
                                        start=(t == 0), stop=(t == 1))
                    ins.then_inc(w_ps, 1)

                def gather_next():
                    pe.wait_ge(w_out_s, n + 1)
                    gather(2 * n + 4)
                    turn_e(CH - 1, 0)

                pe.wait_ge(ue_hi_out, 2 * n + 2)
                pe.wait_ge(ue_lo_out, 2 * n + 2)
                gate_up_e(0, MOE0, 0, 0, 0, False)
                gate_up_e(0, MOE0 + 1, 1, 0, 1, False)
                pe.wait_ge(e_yhi, n + 1)
                pe.wait_ge(e_ylo, n + 1)
                scatter(0)
                scatter(1)
                steps(0, 0, before_up=scatter_rest, before_down=slots_of_this, start=True)
                steps(0, 1, start=True)
                with pe.Fori(1, CH // 2 - 1) as i:
                    steps(i, 0)
                    steps(i, 1)
                steps(CH // 2 - 1, 0)
                steps(CH // 2 - 1, 1, before_down=gather_next)
                down_e(CH - 1, MOE0 + EU - 1, 2, 0, False, True)
            pe.wait_ge(e_yhi, n_visits + 1)
            pe.wait_ge(e_ylo, n_visits + 1)
            for i in range(4):
                if i == 0:
                    pe.wait_ge(ue_lo_out, n_visits * 2 + 2)
                if i >= 2:
                    pe.wait_ge(e_add, n_visits * 4 + i)
                scatter(i)


def unit_arrays(i):
    w_in = i["w_in"]
    col = {"z": 0, "xbc": D, "q": 2 * D + 272, "k": 2 * D + 784, "v": 2 * D + 1296,
           "ga": 2 * D + 1808, "gb": 3 * D + 1808}
    own = {"ssdo": "w_ssd_o", "wout": "w_out", "xk": "xa_wk", "xv": "xa_wv", "xq": "xa_wq",
           "sbo": "w_sb_o", "xo": "xa_wo"}

    def blocks(m, rows, cols, width):
        m = m[rows[0]:rows[1], cols:cols + width]
        return m.reshape(-1, P, width).transpose(1, 0, 2).reshape(P, UNIT)

    def mix_unit(l, name, j):
        if name in col:
            return blocks(w_in[l], (0, D), col[name] + 256 * j, 256)
        m = i[own[name]][l]
        width = UNIT * P // m.shape[0]
        return blocks(m, (0, m.shape[0]), width * j, width)

    def ffn_units(g, u, d):
        gate = [blocks(g, (0, D), 256 * c, 256) for c in range(CH)]
        up = [blocks(u, (0, D), 256 * c, 256) for c in range(CH)]
        dn = [blocks(d, (256 * c, 256 * c + 256), 0, D) for c in range(CH)]
        out = [gate[0], up[0]]
        for c in range(CH - 1):
            out += [gate[c + 1], up[c + 1], dn[c]]
        return out + [dn[CH - 1]]

    out = [mix_unit(0, *m) for m in MIX] + ffn_units(i["ffn_w_gate"][0], i["ffn_w_up"][0], i["ffn_w_down"][0])
    out += [mix_unit(1, *m) for m in MIX]
    for e in range(NE):
        out += ffn_units(i["moe_w_gate"][0, e], i["moe_w_up"][0, e], i["moe_w_down"][0, e])
    assert len(out) == NUNITS
    return np.stack(out)


def kernel(**inputs):
    import concourse.bacc as bacc
    from concourse.bass_utils import run_bass_kernel_spmd

    i = {k: np.asarray(v) for k, v in inputs.items()}

    def columns(v):
        return v.reshape(-1, P).T

    norms = ("norm_mix", "ssd_norm", "norm_mem", "norm_xa", "norm_ffn")
    arrays = {
        "x": i["x"][0], "mem": i["mem"][0], "units": unit_arrays(i),
        "w_dt": np.stack([i["w_in"][l][:, 2 * D + 256:2 * D + 272].reshape(KD, P, 16).transpose(1, 0, 2).reshape(P, -1)
                          for l in range(DEPTH)]),
        "w_router": i["moe_router"][0].reshape(KD, P, NE).transpose(1, 0, 2).reshape(P, -1),
        "gains": np.concatenate([columns(i[n][l]) for l in range(DEPTH) for n in norms], 1),
        "convw": np.concatenate([np.stack([columns(v) for v in (*i["conv_w"][l], i["conv_b"][l])], 2).reshape(P, -1)
                                 for l in range(DEPTH)], 1),
        "rows": np.concatenate([np.concatenate([i["dt_bias"][l], i["a_log"][l], i["d_skip"][l]]) for l in range(DEPTH)]),
        "ffn_row": i["norm_ffn"][1], "final_row": i["final_norm"],
    }
    arrays = {k: np.ascontiguousarray(v) for k, v in arrays.items()}
    nc = bacc.Bacc("TRN2", target_bir_lowering=False, num_devices=1)
    aps = [nc.dram_tensor(k, v.shape, mybir.dt.from_np(v.dtype), kind="ExternalInput").ap() for k, v in arrays.items()]
    out = nc.dram_tensor("out", (S, D), F32, kind="ExternalOutput").ap()
    trunk(nc, *aps, out)
    r = run_bass_kernel_spmd(nc, [arrays], core_ids=[0])
    return r.results[0]["out"].reshape(1, S, D)
```
